# Optimizing a Trainium2 kernel written in Bass

```python
import jax, jax.numpy as jnp
from jax import lax
import numpy as np

D_MODEL = 1024
BATCH = 1
SEQ = 1024
DEPTH = 1

D_PLE = 256
GLA_HEADS = 4
GLA_DK = 64
GLA_DV = 128
GLA_KEY = GLA_HEADS * GLA_DK
GLA_VAL = GLA_HEADS * GLA_DV
GLA_GATE_RANK = 16
GLA_GATE_NORM = 16.0
GLA_CHUNK = 64
POOL_WINDOWS = (2, 4, 8, 16)
POOL_GROUPS = len(POOL_WINDOWS)
POOL_WIDTH = D_MODEL - GLA_VAL
POOL_GC = POOL_WIDTH // POOL_GROUPS
D_MIX = GLA_VAL + POOL_WIDTH
D_IN = 2 * GLA_KEY + 2 * GLA_VAL + GLA_GATE_RANK + POOL_WIDTH
D_FF = ((8 * D_MODEL + 3 * 256 - 1) // (3 * 256)) * 256
EPS = 1e-6

kernel_name = "hybrid_gla_multiscale_pool_block"

def rmsnorm(x, g):
    xf = x.astype(jnp.float32)
    y = xf * lax.rsqrt(jnp.mean(xf * xf, axis=-1, keepdims=True) + EPS)
    return (y * g.astype(jnp.float32)).astype(x.dtype)

def gla_chunked(q, k, v, gk):
    B, T, H, DK = q.shape
    DV = v.shape[-1]
    C = GLA_CHUNK
    N = T // C

    def to_chunks(a):
        return a.astype(jnp.float32).reshape(B, N, C, H, a.shape[-1]).transpose(1, 0, 3, 2, 4)

    qc = to_chunks(q) * (DK ** -0.5)
    kc = to_chunks(k)
    vc = to_chunks(v)
    bc = jnp.cumsum(to_chunks(gk), axis=3)
    mask = jnp.tril(jnp.ones((C, C), dtype=bool))[:, :, None]

    def step(S, inp):
        qi, ki, vi, bi = inp
        diff = bi[:, :, :, None, :] - bi[:, :, None, :, :]
        decay = jnp.exp(jnp.where(mask, diff, -jnp.inf))
        attn = jnp.einsum('bhid,bhjd,bhijd->bhij', qi, ki, decay)
        o = jnp.einsum('bhij,bhjv->bhiv', attn, vi) + \
            jnp.einsum('bhid,bhdv->bhiv', qi * jnp.exp(bi), S)
        b_last = bi[:, :, -1, :]
        S = jnp.exp(b_last)[..., None] * S + jnp.einsum(
            'bhjd,bhjv->bhdv', ki * jnp.exp(b_last[:, :, None, :] - bi), vi)
        return S, o

    S0 = jnp.zeros((B, H, DK, DV), jnp.float32)
    _, o = lax.scan(step, S0, (qc, kc, vc, bc))
    return o.transpose(1, 0, 3, 2, 4).reshape(B, T, H, DV)

def multiscale_pool(u, w_pool, pool_scale):
    B, T, _ = u.shape
    uf = u.astype(jnp.float32).reshape(B, T, POOL_GROUPS, POOL_GC)
    cs = jnp.cumsum(uf, axis=1)
    t = jnp.arange(T)
    outs = []
    for gi, w in enumerate(POOL_WINDOWS):
        c = cs[:, :, gi]
        prev = jnp.pad(c, ((0, 0), (w, 0), (0, 0)))[:, :T]
        cnt = jnp.minimum(t + 1, w).astype(jnp.float32)[None, :, None]
        outs.append((c - prev) / cnt - uf[:, :, gi])
    pooled = jnp.stack(outs, axis=2)
    y = jnp.einsum('btgc,gcd->btgd', pooled, w_pool.astype(jnp.float32))
    y = y.reshape(B, T, POOL_WIDTH) * pool_scale.astype(jnp.float32)
    return y.astype(u.dtype)

def setup_inputs(seed: int = 0) -> dict:
    key = jax.random.key(seed)
    ks = jax.random.split(key, 20)
    f32 = jnp.float32

    def nrm(k, shape, fan_in):
        return jax.random.normal(k, shape, f32) * (fan_in ** -0.5)

    def gain(k, shape):
        return 1.0 + 0.02 * jax.random.normal(k, shape, f32)

    return {
        "x": jax.random.normal(ks[0], (BATCH, SEQ, D_MODEL), f32),
        "p": jax.random.normal(ks[1], (DEPTH, BATCH, SEQ, D_PLE), f32),
        "ln_mix": gain(ks[2], (DEPTH, D_MODEL)),
        "w_in": nrm(ks[3], (DEPTH, D_MODEL, D_IN), D_MODEL),
        "w_gate_lr": nrm(ks[4], (DEPTH, GLA_GATE_RANK, GLA_KEY), GLA_GATE_RANK),
        "b_gate": 0.1 * jax.random.normal(ks[5], (DEPTH, GLA_KEY), f32),
        "gla_norm": gain(ks[6], (DEPTH, GLA_DV)),
        "w_pool": nrm(ks[7], (DEPTH, POOL_GROUPS, POOL_GC, POOL_GC), POOL_GC),
        "pool_scale": gain(ks[8], (DEPTH, POOL_WIDTH)),
        "w_out": nrm(ks[9], (DEPTH, D_MIX, D_MODEL), D_MIX),
        "ln_ffn": gain(ks[10], (DEPTH, D_MODEL)),
        "w_ffn_gate": nrm(ks[11], (DEPTH, D_MODEL, D_FF), D_MODEL),
        "w_ffn_up": nrm(ks[12], (DEPTH, D_MODEL, D_FF), D_MODEL),
        "w_ffn_down": nrm(ks[13], (DEPTH, D_FF, D_MODEL), D_FF),
        "ln_ple": gain(ks[14], (DEPTH, D_MODEL)),
        "w_ple_gate": nrm(ks[15], (DEPTH, D_MODEL, D_MODEL), D_MODEL),
        "w_ple_proj": nrm(ks[16], (DEPTH, D_PLE, D_MODEL), D_PLE),
        "ln_final": gain(ks[17], (D_MODEL,)),
    }

def reference(x, p, ln_mix, w_in, w_gate_lr, b_gate, gla_norm, w_pool, pool_scale,
              w_out, ln_ffn, w_ffn_gate, w_ffn_up, w_ffn_down, ln_ple, w_ple_gate,
              w_ple_proj, ln_final):
    B, T, _ = x.shape
    splits = np.cumsum([GLA_KEY, GLA_KEY, GLA_VAL, GLA_VAL, GLA_GATE_RANK]).tolist()
    h = x
    for i in range(DEPTH):
        a = rmsnorm(h, ln_mix[i])
        z = a @ w_in[i]
        q, k, v, g_out, g_lr, u = jnp.split(z, splits, axis=-1)
        gk = jax.nn.log_sigmoid((g_lr @ w_gate_lr[i] + b_gate[i]).astype(jnp.float32)) / GLA_GATE_NORM
        o = gla_chunked(q.reshape(B, T, GLA_HEADS, GLA_DK),
                        k.reshape(B, T, GLA_HEADS, GLA_DK),
                        v.reshape(B, T, GLA_HEADS, GLA_DV),
                        gk.reshape(B, T, GLA_HEADS, GLA_DK))
        o = rmsnorm(o, gla_norm[i]).reshape(B, T, GLA_VAL).astype(h.dtype)
        o = o * jax.nn.silu(g_out)
        y_pool = multiscale_pool(u, w_pool[i], pool_scale[i])
        mix = jnp.concatenate([o, y_pool], axis=-1) @ w_out[i]
        h = h + mix
        f = rmsnorm(h, ln_ffn[i])
        h = h + (jax.nn.silu(f @ w_ffn_gate[i]) * (f @ w_ffn_up[i])) @ w_ffn_down[i]
        e = rmsnorm(h, ln_ple[i])
        h = h + jax.nn.sigmoid(e @ w_ple_gate[i]) * (p[i].astype(h.dtype) @ w_ple_proj[i])
    return rmsnorm(h, ln_final)


_drawn_inputs = setup_inputs


def setup_inputs(seed=0):
    import zlib

    import numpy as np

    out = dict(_drawn_inputs(seed))
    spreads = {}
    factors = {'ln_mix': 3.132,
     'b_gate': 3.434,
     'gla_norm': 66.372,
     'pool_scale': 59.291,
     'ln_ffn': 13.971,
     'ln_ple': 200.0,
     'ln_final': 23.755,
     'w_ple_gate': 24.136,
     'p': 8.0,
     'w_ple_proj': 8.0}
    for name, (base, spread) in spreads.items():
        noise = np.random.default_rng([zlib.crc32(name.encode()), seed]).standard_normal(out[name].shape)
        drawn = base * np.exp(spread * noise) if base else spread * noise
        out[name] = __import__('jax').numpy.asarray(drawn.astype(out[name].dtype))
    for name, factor in factors.items():
        out[name] = (out[name] * factor).astype(out[name].dtype)
    return out
```

```python
from contextlib import ExitStack

import concourse.bass as bass
from concourse import mybir

F32 = mybir.dt.float32
F32R = mybir.dt.float32r
U32 = mybir.dt.uint32
ALU = mybir.AluOpType
ACT = mybir.ActivationFunctionType

P = 128
T = 1024
D = 1024
KT = D // P
TC = 512
NC = T // TC
C = 128
NCH = T // C
HEADS, DK, DV = 4, 64, 128
KEY, VAL = HEADS * DK, HEADS * DV
KP = KEY // P
RANK = 16
PLE = 256
FF = 2816
BW = 256
BT = BW // P
WINDOWS = (2, 4, 8, 16)
NG = len(WINDOWS)
EPS = 1e-6
LEVELS = (64, 32, 16, 8, 4, 2, 1)
GROUPS = FF // BW
KB = 1024

OFF_V, OFF_G, OFF_LR = 2 * KEY, 2 * KEY + VAL, 2 * KEY + 2 * VAL
OFF_U = OFF_LR + RANK
Z_Q, Z_K, Z_V, Z_U, Z_G = 0, 2, 4, 8, 12
BLOCKS_IN = [(OFF_LR, 1, None), (KEY, 2, Z_K), (0, 2, Z_Q), (OFF_V, 2, Z_V), (OFF_V + BW, 2, Z_V + 2),
             (OFF_U, 2, Z_U), (OFF_U + BW, 2, Z_U + 2), (OFF_G, 2, Z_G), (OFF_G + BW, 2, Z_G + 2)]
B_K, B_Q, B_FIRST_LEVEL = 1, 2, 3
NB = len(BLOCKS_IN)
BLOCK_AT = [sum(KT * P * tiles for _, tiles, _ in BLOCKS_IN[:b]) for b in range(NB + 1)]


def const_rows():
    import numpy as np

    ident = np.eye(P, dtype=np.float32)
    tri = np.triu(np.ones((P, P), np.float32)) / 16.0
    masks = []
    for s in LEVELS:
        m = np.zeros((P, P // (2 * s), s), np.float32)
        for j in range(P):
            if j % (2 * s) < s:
                m[j, j // (2 * s), :] = 1.0
        masks.append(m.reshape(P, P // 2))
    inv = np.tile(1.0 / np.arange(1, 17, dtype=np.float32), (P, 1))
    return np.ascontiguousarray(np.concatenate([ident, tri] + masks + [inv], axis=1))


def hybrid_block(nc, x_t, p_t, gains_in, w_in, w_gate_lr, b_gate, w_pool, w_out, w_ffn_gate, w_ffn_up,
                 w_ffn_down, w_ple_gate, w_ple_proj, consts, out):
    ctx = ExitStack()
    with ctx:
        A0 = 2 * KB
        B0, H0, W0, S0 = A0 + 64 * KB, A0 + 128 * KB, A0 + 160 * KB, A0 + 208 * KB

        def at(name, shape, offset, dt=F32):
            return nc.alloc_sbuf_tensor_at(name, shape, dt, offset=offset)

        a_hi = at("a_hi", [P, KT, T], A0, F32R)
        a_lo = at("a_lo", [P, KT, T], A0 + 32 * KB, F32R)
        mix_hi = at("mix_hi", [P, KT, T], A0, F32R)
        mix_lo = at("mix_lo", [P, KT, T], A0 + 32 * KB, F32R)
        state = at("state", [P, NCH, KP, 2 * DV], A0)
        v_tok = at("v_tok", [P, NCH, VAL], A0 + 32 * KB)
        sum_b = at("sum_b", [P, 3, T], A0 + 48 * KB)
        gu_hi = at("gu_hi", [P, BT, T], A0 + 24 * KB, F32R)
        gu_lo = at("gu_lo", [P, BT, T], A0 + 32 * KB, F32R)
        p_raw = at("p_raw", [P, PLE // P, T], A0 + 40 * KB)
        gate_t = at("gate_t", [P, 2, TC], A0 + 48 * KB)
        up_t = at("up_t", [P, 2, TC], A0 + 52 * KB)
        ple_t = at("ple_t", [P, 2, TC], A0 + 40 * KB)
        p_hi = at("p_hi", [P, PLE // P, T], A0 + 48 * KB, F32R)
        p_lo = at("p_lo", [P, PLE // P, T], A0 + 56 * KB, F32R)
        z = at("z", [P, 16, T], B0)
        pre = at("pre", [P, NCH, KEY], B0 + 48 * KB)
        soft = at("soft", [P, NCH, KEY], B0 + 56 * KB)
        decay = at("decay", [P, KP, T], B0 + 56 * KB)
        lr = at("lr", [RANK + 1, T], B0 + 16 * KB)
        tri = at("tri", [P, P], B0 + 20 * KB)
        w_gl = at("w_gl", [RANK + 1, KEY], B0 + 21 * KB)
        sum_a = at("sum_a", [P, NG, T], B0 + 16 * KB)
        o_tok = at("o_tok", [P, NCH, VAL], B0 + 16 * KB)
        f_hi = at("f_hi", [P, KT, T], B0, F32R)
        f_lo = at("f_lo", [P, KT, T], B0 + 32 * KB, F32R)
        e_hi = at("e_hi", [P, KT, T], B0, F32R)
        e_lo = at("e_lo", [P, KT, T], B0 + 32 * KB, F32R)
        h = at("h", [P, KT, T], H0)
        scaled = at("scaled", [P, 2, KP * T], H0)
        attn = at("attn", [P, 2, NCH, KP, C], H0 + 16 * KB)
        k_tok = at("k_tok", [P, NCH, KEY], H0)
        slot_at = [W0, W0 + 24 * KB, A0]
        w_raw = [at(f"w_raw{s}", [P, KT * BW], o) for s, o in enumerate(slot_at)]
        w_hi = [at(f"w_hi{s}", [P, KT * BW], o + 8 * KB, F32R) for s, o in enumerate(slot_at)]
        w_lo = [at(f"w_lo{s}", [P, KT * BW], o + 16 * KB, F32R) for s, o in enumerate(slot_at)]
        small = [S0]

        def sm(name, shape, dt=F32):
            t = at(name, shape, small[0], dt)
            n = 4
            for d in shape[1:]:
                n *= d
            small[0] += (n + 31) // 32 * 32
            return t

        rms_all = sm("rms_all", [P, T])
        sums = sm("sums", [P, T])
        ident = sm("ident", [P, P])
        masks = sm("masks", [P, len(LEVELS), P // 2])
        inv_t = sm("inv_t", [P, 16])
        ones = sm("ones", [P, P])
        w_pl_at = small[0]
        w_pl = sm("w_pl", [P, NG, P])
        head_t = sm("head_t", [P, 16])
        gains_all = sm("gains_all", [P, 4 * KT + NG + 1])
        gains = gains_all[:, 0:4 * KT].rearrange("p (n k) -> p n k", k=KT)
        g_pool, g_gla = gains_all[:, 4 * KT:4 * KT + NG], gains_all[:, 4 * KT + NG:4 * KT + NG + 1]
        stat = sm("stat", [P, 4, KT])
        o_stat = sm("o_stat", [P, 3, NCH * HEADS])
        last = sm("last", [P, KP, NCH])
        assert small[0] <= nc.sbuf_usable_end, small[0]
        squares = at("squares", [P, TC], w_pl_at)

        pb = [ctx.enter_context(nc.psum_tensor(f"pb{i}", [P, TC], F32)) for i in range(8)]

        def sem(name):
            return ctx.enter_context(nc.semaphore(name))

        class Ring:

            def __init__(self, name, first):
                self.filled, self.drained, self.first = sem(name + "_filled"), sem(name + "_drained"), first

            def bank(self, n):
                return pb[self.first + n % 4]

            def claim(self, n):
                if not isinstance(n, int) or n >= 4:
                    nc.tensor.wait_ge(self.drained, n - 3)

        U_OUT = 2 + 4 * (NB - 1)
        U_FFN = U_OUT + 16
        U_PLE = U_FFN + 8 * GROUPS
        F_NORM1 = 0
        F_GATE = F_NORM1 + 3
        F_DEC = F_GATE + 4
        F_DIAG = F_DEC + 4
        F_LEV = F_DIAG + 8
        F_KT = F_LEV + 4 * len(LEVELS)
        F_VT = F_KT + 4
        F_KV = F_VT + NCH
        F_Y = F_KV + NCH - 1
        F_O = F_Y + 2 * NG
        F_OT = F_O + NCH
        F_NORM2 = F_OT + NCH
        F_DOWN = F_NORM2 + 3
        F_NORM3 = F_DOWN + 16 * GROUPS
        F_NORM4 = F_NORM3 + 3
        proj, aux = Ring("proj", 0), Ring("aux", 4)

        w_landed = [sem(f"w_landed{s}") for s in range(3)]
        w_hi_ready = [sem(f"w_hi_ready{s}") for s in range(3)]
        w_lo_ready = [sem(f"w_lo_ready{s}") for s in range(3)]
        x_landed = [sem(f"x_landed{k}") for k in range(KT)]
        small_landed, gate_w_landed, w_pool_landed, p_landed = (
            sem("small_landed"), sem("gate_w_landed"), sem("w_pool_landed"), sem("p_landed"))
        x_back, out_stored = sem("x_back"), sem("out_stored")
        ones_ready, lr_ones = sem("ones_ready"), sem("lr_ones")
        x_hi_done, x_lo_done, x_sq, x_sum = sem("x_hi_done"), sem("x_lo_done"), sem("x_sq"), sem("x_sum")
        root_ready, recip_ready, diag_ready = sem("root_ready"), sem("recip_ready"), sem("diag_ready")
        soft_ready, log_ready, last_ready = sem("soft_ready"), sem("log_ready"), sem("last_ready")
        diff_ready, exp_ready, scaled_ready, qk_ready = (
            sem("diff_ready"), sem("exp_ready"), sem("scaled_ready"), sem("qk_ready"))
        state_zero, kv_step, silu_ready = sem("state_zero"), sem("kv_step"), sem("silu_ready")
        pool_step, pooled_ready, y_hi = sem("pool_step"), sem("pooled_ready"), sem("y_hi")
        o_squared, o_var, o_root, o_recip, o_scaled, o_hi, o_lo = (
            sem("o_squared"), sem("o_var"), sem("o_root"), sem("o_recip"), sem("o_scaled"), sem("o_hi"), sem("o_lo"))
        f_hi_done, f_lo_done, f_sq, f_sum = sem("f_hi_done"), sem("f_lo_done"), sem("f_sq"), sem("f_sum")
        gate_silu, gu_ready, gu_hi_ready, gu_lo_ready = (
            sem("gate_silu"), sem("gu_ready"), sem("gu_hi_ready"), sem("gu_lo_ready"))
        e_hi_done, e_lo_done, e_sq, e_sum = sem("e_hi_done"), sem("e_lo_done"), sem("e_sq"), sem("e_sum")
        p_hi_done, p_lo_done, ple_sig, h_final, y_sq, y_sum, y_normed = (
            sem("p_hi_done"), sem("p_lo_done"), sem("ple_sig"), sem("h_final"), sem("y_sq"), sem("y_sum"), sem("y_normed"))

        block = ctx.enter_context(nc.Block())

        def both(c):
            return slice(c * TC, (c + 1) * TC)

        USES0, USES1 = (NB + 1) // 2, NB // 2
        OUT0 = (USES0, USES1)
        FFN0 = (USES0 + 2, USES1 + 2, 0)
        PLE0 = (FFN0[0] + GROUPS, FFN0[1] + GROUPS, GROUPS)

        @block.sync
        def _(sp):
            def load(s, n, dst, src):
                if not (isinstance(n, int) and n == 0):
                    sp.wait_ge(w_lo_ready[s], n)
                sp.dma_start(dst, src).then_inc(w_landed[s], 16)

            def in_block(b):
                at_col, n = BLOCK_AT[b], KT * P * BLOCKS_IN[b][1]
                load(b % 2, b // 2, w_raw[b % 2][:, 0:n], w_in[:, at_col:at_col + n])

            sp.dma_start(gains_all[:], gains_in).then_inc(small_landed, 16)
            for k in range(KT):
                sp.dma_start(h[:, k, :], x_t[k]).then_inc(x_landed[k], 16)
                if k == 1:
                    in_block(0)
            in_block(1)
            sp.dma_start(ident[:], consts[:, 0:P]).then_inc(small_landed, 16)
            sp.dma_start(tri[:], consts[:, P:2 * P]).then_inc(gate_w_landed, 16)
            sp.dma_start(w_gl[0:RANK, :], w_gate_lr[0]).then_inc(gate_w_landed, 16)
            sp.dma_start(w_gl[RANK:RANK + 1, :], b_gate).then_inc(gate_w_landed, 16)
            nm = len(LEVELS) * P // 2
            sp.dma_start(masks[:], consts[:, 2 * P:2 * P + nm].rearrange("p (l n) -> p l n", n=P // 2)
                         ).then_inc(gate_w_landed, 16)
            sp.dma_start(inv_t[:], consts[:, 2 * P + nm:]).then_inc(gate_w_landed, 16)
            sp.wait_ge(x_sum, 16)
            sp.dma_start(w_pl[:], w_pool[0].rearrange("g c d -> c g d")).then_inc(w_pool_landed, 16)
            for b in range(2, NB):
                in_block(b)
            for b in range(2):
                load(b % 2, OUT0[b % 2] + b // 2, w_raw[b % 2][:], w_out[b])
            sp.wait_ge(aux.drained, F_O + NCH)
            for k in range(KT):
                sp.dma_start(h[:, k, :], x_t[k]).then_inc(x_back, 16)
            for b in range(2, 4):
                load(b % 2, OUT0[b % 2] + b // 2, w_raw[b % 2][:], w_out[b])

            def ffn_in(i):
                load(0, FFN0[0] + i, w_raw[0][:], w_ffn_gate[bass.ds(i, 1)].rearrange("g p n -> p (g n)"))
                load(1, FFN0[1] + i, w_raw[1][:], w_ffn_up[bass.ds(i, 1)].rearrange("g p n -> p (g n)"))

            def ffn_down(i):
                load(2, i, w_raw[2][:], w_ffn_down[bass.ds(i, 1)].rearrange("g p n -> p (g n)"))

            ffn_in(0)
            sp.wait_ge(proj.filled, U_FFN)
            sp.dma_start(p_raw[:], p_t.rearrange("k p t -> p k t")).then_inc(p_landed, 16)
            ffn_down(0)
            with sp.Fori(0, GROUPS - 1) as i:
                ffn_in(i + 1)
                ffn_down(i + 1)
            for b in range(4):
                load(b % 2, PLE0[b % 2] + b // 2, w_raw[b % 2][:], w_ple_gate[b])
                load(2, PLE0[2] + b, w_raw[2][:, 0:2 * BW], w_ple_proj[b])
            for k in range(KT):
                sp.wait_ge(y_normed, 2 * (k + 1))
                sp.dma_start(out[k], h[:, k, :]).then_inc(out_stored, 16)
            sp.wait_ge(out_stored, 16 * KT)

        @block.gpsimd
        def _(pool):
            def lo_half(s, n, size):
                pool.wait_ge(w_hi_ready[s], n + 1)
                nc.gpsimd.tensor_tensor(w_lo[s][:, 0:size], w_raw[s][:, 0:size], w_hi[s][:, 0:size].bitcast(F32),
                                        ALU.subtract).then_inc(w_lo_ready[s], 1)

            nc.gpsimd.memset(ones[:], 1.0).then_inc(ones_ready, 1)
            nc.gpsimd.memset(lr[:], 1.0).then_inc(lr_ones, 1)
            for b in range(NB):
                lo_half(b % 2, b // 2, KT * P * BLOCKS_IN[b][1])
            for b in range(4):
                lo_half(b % 2, OUT0[b % 2] + b // 2, KT * BW)
            with pool.Fori(0, GROUPS) as i:
                for s in range(3):
                    lo_half(s, FFN0[s] + i, KT * BW)
            for b in range(4):
                lo_half(b % 2, PLE0[b % 2] + b // 2, KT * BW)
                lo_half(2, PLE0[2] + b, 2 * BW)

        @block.scalar
        def _(act):
            def hi_weights(s, n, size, used=None):
                act.wait_ge(w_landed[s], n * 16 + 16)
                if used is not None:
                    act.wait_ge(*used)
                nc.scalar.copy(w_hi[s][:, 0:size], w_raw[s][:, 0:size]).then_inc(w_hi_ready[s], 1)

            def in_block(b):
                if b < NB:
                    hi_weights(b % 2, b // 2, KT * P * BLOCKS_IN[b][1], (proj.filled, 2 + 4 * (b - 2)) if b >= 2 else None)
                elif b < NB + 4:
                    o = b - NB
                    former = U_OUT + 4 * (o - 1) if o >= 2 else U_OUT - 4 * o_first(o)
                    hi_weights(o % 2, OUT0[o % 2] + o // 2, KT * BW, (proj.filled, former))

            def o_first(o):
                return 0 if (NB - 1) % 2 == o else 1

            def root(sem_, value):
                act.wait_ge(sem_, value)
                nc.scalar.activation(stat[:, 1, :], stat[:, 0, :], ACT.Sqrt).then_inc(root_ready, 1)

            def feed(n, m, c, ready, gain, hi, hi_sem, sq_sem, sum_sem):
                act.wait_ge(*ready)
                if gain is not None:
                    nc.scalar.activation(hi[:, m, both(c)], h[:, m, both(c)], ACT.Copy,
                                         scale=gains[:, gain, m:m + 1]).then_inc(hi_sem, 1)
                if n:
                    act.wait_ge(sum_sem, n)
                nc.scalar.activation(squares[:], h[:, m, both(c)], ACT.Square).then_inc(sq_sem, 1)

            act.wait_ge(small_landed, 32)
            for n in range(16):
                if n == 4:
                    in_block(0)
                feed(n, n // NC, n % NC, (x_landed[n // NC], 16), 0, a_hi, x_hi_done, x_sq, x_sum)
            in_block(1)
            root(aux.drained, F_NORM1 + 1)
            in_block(2)
            act.wait_ge(aux.drained, F_GATE + 4)
            nc.scalar.activation(soft[:], pre[:], ACT.Abs).then_inc(soft_ready, 1)
            act.wait_ge(soft_ready, 1)
            nc.scalar.activation(soft[:], soft[:], ACT.Exp, scale=-1.0).then_inc(soft_ready, 1)
            act.wait_ge(soft_ready, 2)
            nc.scalar.activation(soft[:], soft[:], ACT.Ln, bias=1.0).then_inc(soft_ready, 1)
            in_block(3)
            act.wait_ge(aux.drained, F_DEC + 4)
            nc.scalar.activation(last[:], decay[:].rearrange("p a (t c) -> p a t c", c=C)[:, :, :, C - 1], ACT.Exp
                                 ).then_inc(last_ready, 1)
            for lev in range(len(LEVELS)):
                act.wait_ge(diff_ready, 2 * (lev + 1))
                nc.scalar.activation(scaled[:, lev % 2, :], scaled[:, lev % 2, :], ACT.Exp).then_inc(exp_ready, 1)
                in_block(B_FIRST_LEVEL + lev + 1)
            act.wait_ge(diff_ready, 2 * len(LEVELS) + 1)
            nc.scalar.activation(scaled[:, 1, :], scaled[:, 1, :], ACT.Exp).then_inc(exp_ready, 1)
            act.wait_ge(aux.filled, F_KT)
            nc.scalar.activation(scaled[:, 0, :], decay[:].rearrange("p a t -> p (a t)"), ACT.Exp).then_inc(exp_ready, 1)
            act.wait_ge(proj.drained, U_OUT)
            nc.scalar.activation(z[:, Z_G:Z_G + HEADS, :], z[:, Z_G:Z_G + HEADS, :], ACT.Silu).then_inc(silu_ready, 1)
            for n in range(2 * NG):
                g, c = n // NC, n % NC
                act.wait_ge(aux.filled, F_Y + n + 1)
                act.wait_ge(pooled_ready, 2 * NG)
                nc.scalar.activation(mix_hi[:, HEADS + g, both(c)], aux.bank(F_Y + n)[:], ACT.Copy,
                                     scale=g_pool[:, g:g + 1]).then_inc(y_hi, 1)
            for t in range(NCH):
                act.wait_ge(aux.drained, F_O + t + 1)
                if t >= 2:
                    act.wait_ge(o_squared, t - 1)
                for hd in range(HEADS):
                    sq_at = (t % 2 * HEADS + hd) * DV
                    i = nc.scalar.activation(sums[:, sq_at:sq_at + DV], o_tok[:, t, hd * DV:(hd + 1) * DV], ACT.Square,
                                             accum_out=o_stat[:, 0, t * HEADS + hd:t * HEADS + hd + 1])
                i.then_inc(o_squared, 1)
            act.wait_ge(o_var, 1)
            nc.scalar.activation(o_stat[:, 2, :], o_stat[:, 1, :], ACT.Sqrt).then_inc(o_root, 1)
            for t in range(NCH):
                act.wait_ge(aux.drained, F_OT + t + 1)
                nc.scalar.activation(mix_hi[:, 0:HEADS, t * C:(t + 1) * C],
                                     o_tok[:, t, :].rearrange("p (h c) -> p h c", c=C), ACT.Copy).then_inc(o_hi, 1)

            for n in range(16):
                if n in (4, 8):
                    in_block(NB + 1 + n // 4)
                if n == 12:
                    hi_weights(0, FFN0[0], KT * BW, (proj.filled, U_OUT + 12))
                feed(n, n // NC, n % NC, (proj.drained, U_OUT + n + 1), 1, f_hi, f_hi_done, f_sq, f_sum)
            hi_weights(1, FFN0[1], KT * BW, (proj.filled, U_FFN))
            root(aux.drained, F_NORM2 + 1)
            hi_weights(2, FFN0[2], KT * BW)

            def ffn_pair(i, n):
                act.wait_ge(proj.drained, i * 8 + (U_FFN + 2 * n + 1))
                nc.scalar.activation(gate_t[:, n % 2, :], gate_t[:, n % 2, :], ACT.Silu).then_inc(gate_silu, 1)
                act.wait_ge(gu_ready, i * 4 + (n + 1))
                nc.scalar.copy(gu_hi[:, n // 2, both(n % 2)], up_t[:, n % 2, :]).then_inc(gu_hi_ready, 1)

            with act.Fori(0, GROUPS - 1) as i:
                for n in range(4):
                    ffn_pair(i, n)
                hi_weights(0, i + (FFN0[0] + 1), KT * BW, (proj.filled, i * 8 + (U_FFN + 7)))
                hi_weights(1, i + (FFN0[1] + 1), KT * BW, (proj.filled, i * 8 + (U_FFN + 8)))
                hi_weights(2, i + 1, KT * BW, (aux.filled, i * 16 + (F_DOWN + 16)))
            for n in range(4):
                ffn_pair(GROUPS - 1, n)
            hi_weights(0, PLE0[0], KT * BW, (proj.filled, U_PLE - 1))
            hi_weights(1, PLE0[1], KT * BW, (proj.filled, U_PLE))
            for n in range(16):
                feed(n, n % KT, n // KT, (aux.drained, F_NORM3 - 16 + n + 1), 2, e_hi, e_hi_done, e_sq, e_sum)
            hi_weights(2, PLE0[2], 2 * BW, (aux.filled, F_NORM3))
            act.wait_ge(p_landed, 16)
            for k in range(PLE // P):
                nc.scalar.copy(p_hi[:, k, :], p_raw[:, k, :]).then_inc(p_hi_done, 1)
            root(aux.drained, F_NORM3 + 1)
            for n in range(16):
                b = n // 4
                if n % 4 == 0 and b > 0:
                    hi_weights(2, PLE0[2] + b, 2 * BW, (proj.filled, U_PLE + 8 * b))
                    if b < 3:
                        hi_weights((b + 1) % 2, PLE0[(b + 1) % 2] + (b + 1) // 2, KT * BW, (proj.filled, U_PLE + 8 * b - 1))
                act.wait_ge(proj.drained, U_PLE + 2 * n + 1)
                nc.scalar.activation(ple_t[:, n % 2, :], ple_t[:, n % 2, :], ACT.Sigmoid).then_inc(ple_sig, 1)
                feed(n, n // NC, n % NC, (h_final, n + 1), None, None, None, y_sq, y_sum)
            root(aux.drained, F_NORM4 + 1)

        @block.vector
        def _(dve):
            V = nc.vector

            def diagonal(n):
                dve.wait_ge(root_ready, n)
                V.reciprocal(stat[:, 3, :], stat[:, 1, :]).then_inc(recip_ready, 1)
                dve.wait_ge(recip_ready, n)
                V.tensor_tensor(sums[:].rearrange("p (t c) -> p t c", c=P),
                                ident[:].unsqueeze(1).broadcast_to([P, NCH, P]),
                                stat[:, 3, :].unsqueeze(2).broadcast_to([P, NCH, P]), ALU.mult).then_inc(diag_ready, 1)

            def take_rms(f0):
                for c in range(NC):
                    dve.wait_ge(aux.filled, f0 + c + 1)
                    V.tensor_copy(rms_all[:, both(c)], aux.bank(f0 + c)[:]).then_inc(aux.drained, 1)
                dve.wait_ge(aux.drained, f0 + NC)

            def feed(n, m, c, gain, hi, lo, hi_sem, lo_sem, sq_sem, sum_sem):
                if gain is not None:
                    dve.wait_ge(hi_sem, n + 1)
                    V.scalar_tensor_tensor(out=lo[:, m, both(c)], in0=h[:, m, both(c)], scalar=gains[:, gain, m:m + 1],
                                           in1=hi[:, m, both(c)].bitcast(F32), op0=ALU.mult,
                                           op1=ALU.subtract).then_inc(lo_sem, 1)
                dve.wait_ge(sq_sem, n + 1)
                if m == 0:
                    V.tensor_copy(sums[:, both(c)], squares[:]).then_inc(sum_sem, 1)
                else:
                    dve.wait_ge(sum_sem, n)
                    V.tensor_tensor(sums[:, both(c)], sums[:, both(c)], squares[:], ALU.add).then_inc(sum_sem, 1)

            def norm_stats(f0, n):
                dve.wait_ge(aux.filled, f0 + 1)
                V.tensor_scalar(stat[:, 0, :], aux.bank(f0)[:, 0:KT], 1.0 / D, EPS, ALU.mult, ALU.add
                                ).then_inc(aux.drained, 1)
                diagonal(n)
                take_rms(f0 + 1)

            dve.wait_ge(small_landed, 32)
            for n in range(16):
                dve.wait_ge(x_landed[n // NC], 16)
                feed(n, n // NC, n % NC, 0, a_hi, a_lo, x_hi_done, x_lo_done, x_sq, x_sum)
            norm_stats(F_NORM1, 1)
            dve.wait_ge(gate_w_landed, 16 * 5)

            def z_unit(u, dst):
                n, c = dst
                dve.wait_ge(proj.filled, u + 1)
                V.tensor_tensor(z[:, n, both(c)], proj.bank(u)[:], rms_all[:, both(c)], ALU.mult
                                ).then_inc(proj.drained, 1)

            def z_block(b, part=None):
                for j in range(4) if part is None else part:
                    z_unit(2 + 4 * (b - 1) + j, (BLOCKS_IN[b][2] + j // 2, j % 2))

            dve.wait_ge(lr_ones, 1)
            for c in range(NC):
                dve.wait_ge(proj.filled, c + 1)
                V.tensor_tensor(lr[0:RANK, both(c)], proj.bank(c)[0:RANK, :], rms_all[0:RANK, both(c)], ALU.mult
                                ).then_inc(proj.drained, 1)
            for n in range(4):
                dve.wait_ge(aux.filled, F_GATE + n + 1)
                V.tensor_copy(pre[:, 2 * n:2 * n + 2, :], aux.bank(F_GATE + n)[:].rearrange("p (t n) -> p t n", t=2)
                              ).then_inc(aux.drained, 1)
            z_block(B_K)
            dve.wait_ge(soft_ready, 3)
            V.scalar_tensor_tensor(out=soft[:], in0=pre[:], scalar=0.0, in1=soft[:], op0=ALU.min,
                                   op1=ALU.subtract).then_inc(log_ready, 1)
            for n in range(4):
                dve.wait_ge(aux.filled, F_DEC + n + 1)
                if n == 0:
                    dve.wait_ge(aux.filled, F_DEC + 4)
                V.tensor_copy(decay[:, n // 2, both(n % 2)], aux.bank(F_DEC + n)[:]).then_inc(aux.drained, 1)
            z_block(B_Q)
            dve.wait_ge(aux.drained, F_DEC + 4)
            dve.wait_ge(proj.drained, 2 + 8)

            flat_b = decay[:].rearrange("p a t -> p (a t)")
            flat_k = z[:, Z_K:Z_K + KP, :].rearrange("p a t -> p (a t)")
            flat_q = z[:, Z_Q:Z_Q + KP, :].rearrange("p a t -> p (a t)")

            def halves(ap, s):
                v = ap.rearrange("p (n s) -> p n s", s=2 * s)
                return v[:, :, 0:s], v[:, :, s:2 * s]

            def level_diff(lev):
                s = LEVELS[lev]
                left, right = halves(flat_b, s)
                ref = flat_b.rearrange("p (n s) -> p n s", s=2 * s)[:, :, s - 1:s].broadcast_to([P, KP * T // (2 * s), s])
                o_left, o_right = halves(scaled[:, lev % 2, :], s)
                V.tensor_tensor(o_left, ref, left, ALU.subtract).then_inc(diff_ready, 1)
                V.tensor_tensor(o_right, right, ref, ALU.subtract).then_inc(diff_ready, 1)

            def level_scale(lev):
                s = LEVELS[lev]
                dve.wait_ge(exp_ready, lev + 1)
                o_left, o_right = halves(scaled[:, lev % 2, :], s)
                V.tensor_tensor(o_left, o_left, halves(flat_k, s)[0], ALU.mult).then_inc(scaled_ready, 1)
                V.scalar_tensor_tensor(out=o_right, in0=halves(flat_q, s)[1], scalar=DK ** -0.5, in1=o_right,
                                       op0=ALU.mult, op1=ALU.mult).then_inc(scaled_ready, 1)

            def select(lev):
                s = LEVELS[lev]
                dve.wait_ge(aux.drained, F_LEV + 4 * lev)
                for n in range(4):
                    r, c = n % 2, n // 2
                    f = F_LEV + 4 * lev + n
                    dve.wait_ge(aux.filled, f + 1)
                    dst = attn[:, r, 4 * c:4 * c + 4, :, :].rearrange("p t a (n s) -> p (t a) n s", s=2 * s)[:, :, :, s:2 * s]
                    m = masks[:, lev, :].rearrange("p (n s) -> p n s", s=s).unsqueeze(1).broadcast_to(
                        [P, 4 * KP, C // (2 * s), s])
                    src = aux.bank(f)[:].rearrange("p (a n s) -> p a n s", a=4 * KP, s=s)
                    V.copy_predicated(dst, m.bitcast(U32), src).then_inc(aux.drained, 1)

            def diagonal_attn():
                for n in range(8):
                    r, t2 = n % 2, n // 2
                    dve.wait_ge(aux.filled, F_DIAG + n + 1)
                    V.scalar_tensor_tensor(
                        out=attn[:, r, 2 * t2:2 * t2 + 2, :, :].rearrange("p t a c -> p (t a) c"),
                        in0=aux.bank(F_DIAG + n)[:].rearrange("p (a c) -> p a c", c=C), scalar=DK ** -0.5,
                        in1=ident[:].unsqueeze(1).broadcast_to([P, 2 * KP, C]), op0=ALU.mult, op1=ALU.mult
                    ).then_inc(aux.drained, 1)

            last_level = len(LEVELS) - 1
            for lev in range(last_level):
                b = B_FIRST_LEVEL + lev
                level_diff(lev)
                if b < NB - 1:
                    z_block(b, (0, 1))
                level_scale(lev)
                if b < NB - 1:
                    z_block(b, (2, 3))
                if lev == 0:
                    diagonal_attn()
                if lev == last_level - 1:
                    level_diff(last_level)
                    level_scale(last_level)
                select(lev)
            b4 = decay[:].rearrange("p a (t c) -> p (a t) c", c=C)
            V.tensor_tensor(scaled[:, 1, :].rearrange("p (n c) -> p n c", c=C),
                            b4[:, :, C - 1:C].broadcast_to([P, KP * NCH, C]), b4, ALU.subtract).then_inc(diff_ready, 1)
            select(last_level)
            dve.wait_ge(last_ready, 1)
            dve.wait_ge(exp_ready, len(LEVELS) + 2)
            z_block(NB - 1)
            V.tensor_tensor(flat_k, flat_k, scaled[:, 1, :], ALU.mult).then_inc(qk_ready, 1)
            V.scalar_tensor_tensor(out=flat_q, in0=flat_q, scalar=DK ** -0.5, in1=scaled[:, 0, :], op0=ALU.mult,
                                   op1=ALU.mult).then_inc(qk_ready, 1)
            dve.wait_ge(qk_ready, 2)
            V.memset(state[:], 0.0).then_inc(state_zero, 1)
            for n in range(4):
                dve.wait_ge(aux.filled, F_KT + n + 1)
                V.tensor_copy(k_tok[:, 2 * n:2 * n + 2, :], aux.bank(F_KT + n)[:].rearrange("p (t c) -> p t c", t=2)
                              ).then_inc(aux.drained, 1)
            for t in range(NCH):
                dve.wait_ge(aux.filled, F_VT + t + 1)
                V.tensor_copy(v_tok[:, t, :], aux.bank(F_VT + t)[:]).then_inc(aux.drained, 1)
            dve.wait_ge(state_zero, 1)
            for t in range(NCH - 1):
                f = F_KV + t
                dve.wait_ge(aux.filled, f + 1)
                if t:
                    dve.wait_ge(kv_step, 3 * t)
                    dve.wait_ge(aux.drained, f)
                for a in range(KP):
                    for r in range(2):
                        rows, cols = slice(r * DK, (r + 1) * DK), slice(r * DV, (r + 1) * DV)
                        i = V.scalar_tensor_tensor(
                            out=state[rows, t + 1, a, cols], in0=state[rows, t, a, cols],
                            scalar=last[rows, a, t:t + 1],
                            in1=aux.bank(f)[rows, a * 2 * DV + r * DV:a * 2 * DV + (r + 1) * DV],
                            op0=ALU.mult, op1=ALU.add)
                        i.then_inc(aux.drained if (a, r) == (KP - 1, 1) else kv_step, 1)

            u = z[:, Z_U:Z_U + NG, :]
            steps = [0]

            def step(i):
                steps[0] += 1
                i.then_inc(pool_step, 1)

            def joined():
                dve.wait_ge(pool_step, steps[0])

            cur, first = u, 0
            for g, w in enumerate(WINDOWS):
                sh = w // 2
                new = (sum_a[:, g:NG, :], sum_b[:, g - 1:NG - 1, :])[g % 2]
                src = cur[:, g - first:, :]
                if g:
                    joined()
                step(V.tensor_tensor(new[:, :, sh:T], src[:, :, sh:T], src[:, :, 0:T - sh], ALU.add))
                step(V.tensor_copy(new[:, :, 0:sh], src[:, :, 0:sh]))
                joined()
                V.scalar_tensor_tensor(out=u[:, g, w:T], in0=new[:, 0, w:T], scalar=1.0 / w, in1=u[:, g, w:T],
                                       op0=ALU.mult, op1=ALU.subtract).then_inc(pooled_ready, 1)
                step(V.tensor_tensor(head_t[:, 0:w], new[:, 0, 0:w], inv_t[:, 0:w], ALU.mult))
                joined()
                V.tensor_tensor(u[:, g, 0:w], head_t[:, 0:w], u[:, g, 0:w], ALU.subtract).then_inc(pooled_ready, 1)
                cur, first = new, g
            for n in range(2 * NG):
                g, c = n // NC, n % NC
                dve.wait_ge(y_hi, n + 1)
                V.scalar_tensor_tensor(out=mix_lo[:, HEADS + g, both(c)], in0=aux.bank(F_Y + n)[:],
                                       scalar=g_pool[:, g:g + 1], in1=mix_hi[:, HEADS + g, both(c)].bitcast(F32),
                                       op0=ALU.mult, op1=ALU.subtract).then_inc(aux.drained, 1)
            for t in range(NCH):
                dve.wait_ge(aux.filled, F_O + t + 1)
                V.tensor_copy(o_tok[:, t, :], aux.bank(F_O + t)[:]).then_inc(aux.drained, 1)
            dve.wait_ge(o_squared, NCH)
            V.tensor_scalar(o_stat[:, 1, :], o_stat[:, 0, :], 1.0 / DV, EPS, ALU.mult, ALU.add).then_inc(o_var, 1)
            dve.wait_ge(o_root, 1)
            V.reciprocal(o_stat[:, 1, :], o_stat[:, 2, :]).then_inc(o_recip, 1)
            dve.wait_ge(o_recip, 1)
            for t in range(NCH):
                ov = o_tok[:, t, :].rearrange("p (h c) -> p h c", c=DV)
                V.tensor_tensor(ov, ov, o_stat[:, 1, t * HEADS:(t + 1) * HEADS].unsqueeze(2).broadcast_to([P, HEADS, DV]),
                                ALU.mult).then_inc(o_scaled, 1)
            dve.wait_ge(silu_ready, 1)

            def o_low(t):
                dve.wait_ge(o_hi, t + 1)
                V.tensor_tensor(mix_lo[:, 0:HEADS, t * C:(t + 1) * C], o_tok[:, t, :].rearrange("p (h c) -> p h c", c=C),
                                mix_hi[:, 0:HEADS, t * C:(t + 1) * C].bitcast(F32), ALU.subtract).then_inc(o_lo, 1)

            for t in range(NCH):
                dve.wait_ge(aux.filled, F_OT + t + 1)
                V.scalar_tensor_tensor(
                    out=o_tok[:, t, :].rearrange("p (h c) -> p h c", c=C),
                    in0=aux.bank(F_OT + t)[:].rearrange("p (h c) -> p h c", c=C), scalar=g_gla[:, 0:1],
                    in1=z[:, Z_G:Z_G + HEADS, t * C:(t + 1) * C], op0=ALU.mult, op1=ALU.mult).then_inc(aux.drained, 1)
                if t:
                    o_low(t - 1)
            o_low(NCH - 1)

            dve.wait_ge(x_back, 16 * KT)

            for n in range(16):
                m, c = n // NC, n % NC
                dve.wait_ge(proj.filled, U_OUT + n + 1)
                V.tensor_tensor(h[:, m, both(c)], h[:, m, both(c)], proj.bank(U_OUT + n)[:], ALU.add
                                ).then_inc(proj.drained, 1)
                if n:
                    feed(n - 1, (n - 1) // NC, (n - 1) % NC, 1, f_hi, f_lo, f_hi_done, f_lo_done, f_sq, f_sum)
            feed(15, KT - 1, 1, 1, f_hi, f_lo, f_hi_done, f_lo_done, f_sq, f_sum)
            norm_stats(F_NORM2, 2)

            def ffn_pair(i, n):
                c = n % 2
                dve.wait_ge(proj.filled, i * 8 + (U_FFN + 2 * n + 1))
                V.tensor_tensor(gate_t[:, c, :], proj.bank(U_FFN + 2 * n)[:], rms_all[:, both(c)], ALU.mult
                                ).then_inc(proj.drained, 1)
                dve.wait_ge(proj.filled, i * 8 + (U_FFN + 2 * n + 2))
                V.tensor_tensor(up_t[:, c, :], proj.bank(U_FFN + 2 * n + 1)[:], rms_all[:, both(c)], ALU.mult
                                ).then_inc(proj.drained, 1)
                dve.wait_ge(gate_silu, i * 4 + (n + 1))
                dve.wait_ge(proj.drained, i * 8 + (U_FFN + 2 * n + 2))
                V.tensor_tensor(up_t[:, c, :], gate_t[:, c, :], up_t[:, c, :], ALU.mult).then_inc(gu_ready, 1)
                dve.wait_ge(gu_hi_ready, i * 4 + (n + 1))
                V.tensor_tensor(gu_lo[:, n // 2, both(c)], up_t[:, c, :], gu_hi[:, n // 2, both(c)].bitcast(F32),
                                ALU.subtract).then_inc(gu_lo_ready, 1)

            def ffn_add(i, n):
                m, c = n % KT, n // KT
                dve.wait_ge(aux.filled, i * 16 + (F_DOWN + n + 1))
                V.tensor_tensor(h[:, m, both(c)], h[:, m, both(c)], aux.bank(F_DOWN + n)[:], ALU.add
                                ).then_inc(aux.drained, 1)

            with dve.Fori(0, GROUPS - 1) as i:
                for n in range(4):
                    ffn_pair(i, n)
                for n in range(16):
                    ffn_add(i, n)
            for n in range(4):
                ffn_pair(GROUPS - 1, n)
            for n in range(16):
                ffn_add(GROUPS - 1, n)
                if n:
                    feed(n - 1, (n - 1) % KT, (n - 1) // KT, 2, e_hi, e_lo, e_hi_done, e_lo_done, e_sq, e_sum)
            feed(15, KT - 1, 1, 2, e_hi, e_lo, e_hi_done, e_lo_done, e_sq, e_sum)
            for k in range(PLE // P):
                dve.wait_ge(p_hi_done, k + 1)
                V.tensor_tensor(p_lo[:, k, :], p_raw[:, k, :], p_hi[:, k, :].bitcast(F32), ALU.subtract
                                ).then_inc(p_lo_done, 1)
            norm_stats(F_NORM3, 3)

            for n in range(16):
                m, c = n // NC, n % NC
                u = U_PLE + 2 * n
                dve.wait_ge(proj.filled, u + 1)
                V.tensor_tensor(ple_t[:, n % 2, :], proj.bank(u)[:], rms_all[:, both(c)], ALU.mult
                                ).then_inc(proj.drained, 1)
                dve.wait_ge(proj.filled, u + 2)
                dve.wait_ge(ple_sig, n + 1)
                V.tensor_tensor(ple_t[:, n % 2, :], ple_t[:, n % 2, :], proj.bank(u + 1)[:], ALU.mult
                                ).then_inc(proj.drained, 1)
                dve.wait_ge(proj.drained, u + 2)
                V.tensor_tensor(h[:, m, both(c)], h[:, m, both(c)], ple_t[:, n % 2, :], ALU.add).then_inc(h_final, 1)
                if n:
                    feed(n - 1, (n - 1) // NC, (n - 1) % NC, None, None, None, None, None, y_sq, y_sum)
            feed(15, KT - 1, 1, None, None, None, None, None, y_sq, y_sum)
            norm_stats(F_NORM4, 4)
            for n in range(16):
                m, c = n // NC, n % NC
                V.scalar_tensor_tensor(out=h[:, m, both(c)], in0=h[:, m, both(c)], scalar=gains[:, 3, m:m + 1],
                                       in1=rms_all[:, both(c)], op0=ALU.mult, op1=ALU.mult).then_inc(y_normed, 1)

        @block.tensor
        def _(pe):
            M = nc.tensor.matmul

            def split3(bank, w_h, w_l, x_h, x_l, start, stop):
                M(bank, w_h, x_h, start=start, stop=False)
                M(bank, w_h, x_l, start=False, stop=False)
                return M(bank, w_l, x_h, start=False, stop=stop)

            def unit(n, s, tiles, m, x_h, x_l, c, kts=KT, lo_sem=None):
                wh = w_hi[s][:, 0:kts * tiles * P].rearrange("p (k n) -> p k n", k=kts)
                wl = w_lo[s][:, 0:kts * tiles * P].rearrange("p (k n) -> p k n", k=kts)
                cols = slice(m * P, (m + 1) * P)
                for k in range(kts):
                    if lo_sem is not None:
                        pe.wait_ge(lo_sem, NC * k + c + 1)
                    i = split3(proj.bank(n)[:], wh[:, k, cols], wl[:, k, cols], x_h[:, k, both(c)], x_l[:, k, both(c)],
                               k == 0, k == kts - 1)
                i.then_inc(proj.filled, 1)

            def spread_rms(f0, n):
                pe.wait_ge(diag_ready, n)
                for c in range(NC):
                    aux.claim(f0 + c)
                    M(aux.bank(f0 + c)[:], ones[:], sums[:, both(c)], start=True, stop=True).then_inc(aux.filled, 1)

            def token_sums(f0, ready):
                pe.wait_ge(ready, 16)
                aux.claim(f0)
                for t in range(NCH):
                    i = M(aux.bank(f0)[:, t:t + 1], sums[:, t * P:(t + 1) * P], ones[:, 0:1], start=True, stop=True)
                i.then_inc(aux.filled, 1)

            def in_block(b):
                pe.wait_ge(w_lo_ready[b % 2], b // 2 + 1)
                tiles = BLOCKS_IN[b][1]
                u0 = 0 if b == 0 else 2 + 4 * (b - 1)
                for j in range(2 * tiles):
                    proj.claim(u0 + j)
                    unit(u0 + j, b % 2, tiles, j // 2, a_hi, a_lo, j % 2, lo_sem=x_lo_done if b == 0 else None)

            in_block(0)
            pe.wait_ge(ones_ready, 1)
            token_sums(F_NORM1, x_sum)
            spread_rms(F_NORM1 + 1, 1)
            in_block(B_K)
            pe.wait_ge(proj.drained, 2)
            pe.wait_ge(gate_w_landed, 16 * 5)
            pe.wait_ge(lr_ones, 1)
            for n in range(4):
                aux.claim(F_GATE + n)
                for j in range(2):
                    t = 2 * n + j
                    i = M(aux.bank(F_GATE + n)[:, j * KEY:(j + 1) * KEY], lr[:, t * C:(t + 1) * C], w_gl[:],
                          start=True, stop=True)
                i.then_inc(aux.filled, 1)
            in_block(B_Q)
            pe.wait_ge(log_ready, 1)
            for n in range(4):
                a, c = n // 2, n % 2
                aux.claim(F_DEC + n)
                for j in range(4):
                    i = M(aux.bank(F_DEC + n)[:, j * C:(j + 1) * C], soft[:, 4 * c + j, a * P:(a + 1) * P], tri[:],
                          start=True, stop=True)
                i.then_inc(aux.filled, 1)
            in_block(B_FIRST_LEVEL)
            pe.wait_ge(proj.drained, 2 + 8)
            for n in range(8):
                r, t2 = n % 2, n // 2
                rows = slice(r * DK, (r + 1) * DK)
                aux.claim(F_DIAG + n)
                for j in range(4):
                    t, a = 2 * t2 + j // 2, j % 2
                    i = M(aux.bank(F_DIAG + n)[:, j * C:(j + 1) * C], z[rows, Z_K + a, t * C:(t + 1) * C],
                          z[rows, Z_Q + a, t * C:(t + 1) * C], start=True, stop=True)
                i.then_inc(aux.filled, 1)
            for lev, s in enumerate(LEVELS):
                pe.wait_ge(scaled_ready, 2 * (lev + 1))
                sc = scaled[:, lev % 2, :].rearrange("p (a t c) -> p a t c", a=KP, c=C)
                for n in range(4):
                    r, c = n % 2, n // 2
                    f = F_LEV + 4 * lev + n
                    rows = slice(r * DK, (r + 1) * DK)
                    aux.claim(f)
                    for j in range(4 * KP):
                        t, a = 4 * c + j // KP, j % KP
                        right = sc[rows, a, t, :].rearrange("p (n s) -> p n s", s=2 * s)[:, :, s:2 * s]
                        i = M(aux.bank(f)[:, j * C // 2:(j + 1) * C // 2], sc[rows, a, t, :], right, start=True, stop=True)
                    i.then_inc(aux.filled, 1)
                if B_FIRST_LEVEL + lev + 1 < NB:
                    in_block(B_FIRST_LEVEL + lev + 1)
            pe.wait_ge(small_landed, 32)
            pe.wait_ge(qk_ready, 2)
            for n in range(4):
                aux.claim(F_KT + n)
                for j in range(4):
                    t, a = 2 * n + j // 2, j % 2
                    i = nc.tensor.transpose(aux.bank(F_KT + n)[:, j * P:(j + 1) * P], z[:, Z_K + a, t * C:(t + 1) * C], ident[:])
                i.then_inc(aux.filled, 1)
            for t in range(NCH):
                aux.claim(F_VT + t)
                for hd in range(HEADS):
                    i = nc.tensor.transpose(aux.bank(F_VT + t)[:, hd * P:(hd + 1) * P], z[:, Z_V + hd, t * C:(t + 1) * C], ident[:])
                i.then_inc(aux.filled, 1)
            pe.wait_ge(aux.drained, F_KV)
            for t in range(NCH - 1):
                aux.claim(F_KV + t)
                for a in range(KP):
                    i = M(aux.bank(F_KV + t)[:, a * 2 * DV:(a + 1) * 2 * DV], k_tok[:, t, a * P:(a + 1) * P],
                          v_tok[:, t, a * 2 * DV:(a + 1) * 2 * DV], start=True, stop=True)
                i.then_inc(aux.filled, 1)
            pe.wait_ge(w_pool_landed, 16)
            for n in range(2 * NG):
                g, c = n // NC, n % NC
                if c == 0:
                    pe.wait_ge(pooled_ready, 2 * (g + 1))
                aux.claim(F_Y + n)
                M(aux.bank(F_Y + n)[:], w_pl[:, g, :], z[:, Z_U + g, both(c)], start=True, stop=True
                  ).then_inc(aux.filled, 1)
            pe.wait_ge(kv_step, 3 * (NCH - 1))
            pe.wait_ge(aux.drained, F_Y)
            for t in range(NCH):
                aux.claim(F_O + t)
                bank = aux.bank(F_O + t)
                if t:
                    for a in range(KP):
                        M(bank[:, a * 2 * DV:(a + 1) * 2 * DV], z[:, Z_Q + a, t * C:(t + 1) * C], state[:, t, a, :],
                          start=(a == 0), stop=False, skip_group_check=True)
                for hd in range(HEADS):
                    i = M(bank[:, hd * DV:(hd + 1) * DV], attn[:, hd % 2, t, hd // 2, :], v_tok[:, t, hd * DV:(hd + 1) * DV],
                          start=(t == 0 and hd == 0), stop=(hd == HEADS - 1), skip_group_check=True)
                i.then_inc(aux.filled, 1)
            for t in range(NCH):
                pe.wait_ge(o_scaled, t + 1)
                aux.claim(F_OT + t)
                for hd in range(HEADS):
                    i = nc.tensor.transpose(aux.bank(F_OT + t)[:, hd * P:(hd + 1) * P], o_tok[:, t, hd * DV:(hd + 1) * DV], ident[:])
                i.then_inc(aux.filled, 1)

            pe.wait_ge(aux.drained, F_OT)
            pe.wait_ge(o_lo, NCH)
            for b in range(4):
                pe.wait_ge(w_lo_ready[b % 2], OUT0[b % 2] + b // 2 + 1)
                for j in range(4):
                    n = U_OUT + 4 * b + j
                    proj.claim(n)
                    unit(n, b % 2, BT, j // 2, mix_hi, mix_lo, j % 2)

            token_sums(F_NORM2, f_sum)
            spread_rms(F_NORM2 + 1, 2)
            pe.wait_ge(f_lo_done, 16)
            wd_h = w_hi[2][:].rearrange("p (k n) -> p k n", n=D)
            wd_l = w_lo[2][:].rearrange("p (k n) -> p k n", n=D)
            with pe.Fori(0, GROUPS) as i:
                pe.wait_ge(w_lo_ready[0], i + (FFN0[0] + 1))
                for n in range(4):
                    for s in range(2):
                        if (n, s) == (0, 1):
                            pe.wait_ge(w_lo_ready[1], i + (FFN0[1] + 1))
                        pe.wait_ge(proj.drained, i * 8 + (U_FFN + 2 * n + s - 3))
                        unit(U_FFN + 2 * n + s, s, BT, n // 2, f_hi, f_lo, n % 2)
                pe.wait_ge(w_lo_ready[2], i + 1)
                for n in range(16):
                    m, c = n % KT, n // KT
                    if m == 0:
                        pe.wait_ge(gu_lo_ready, i * 4 + (3 + c))
                    pe.wait_ge(aux.drained, i * 16 + (F_DOWN + n - 3))
                    bank, cols = aux.bank(F_DOWN + n)[:], slice(m * P, (m + 1) * P)
                    for k in range(BT):
                        last_mm = split3(bank, wd_h[:, k, cols], wd_l[:, k, cols], gu_hi[:, k, both(c)],
                                         gu_lo[:, k, both(c)], k == 0, k == BT - 1)
                    last_mm.then_inc(aux.filled, 1)

            token_sums(F_NORM3, e_sum)
            spread_rms(F_NORM3 + 1, 3)
            pe.wait_ge(e_lo_done, 16)
            pe.wait_ge(p_lo_done, PLE // P)
            for b in range(4):
                pe.wait_ge(w_lo_ready[b % 2], PLE0[b % 2] + b // 2 + 1)
                for j in range(4):
                    n = 4 * b + j
                    proj.claim(U_PLE + 2 * n)
                    unit(U_PLE + 2 * n, b % 2, BT, j // 2, e_hi, e_lo, j % 2)
                    if j == 0:
                        pe.wait_ge(w_lo_ready[2], PLE0[2] + b + 1)
                    proj.claim(U_PLE + 2 * n + 1)
                    unit(U_PLE + 2 * n + 1, 2, BT, j // 2, p_hi, p_lo, j % 2, kts=PLE // P)
            token_sums(F_NORM4, y_sum)
            spread_rms(F_NORM4 + 1, 4)


_INS = ['x_t', 'p_t', 'gains_in', 'w_in', 'w_gate_lr', 'b_gate', 'w_pool', 'w_out', 'w_ffn_gate', 'w_ffn_up', 'w_ffn_down',
        'w_ple_gate', 'w_ple_proj', 'consts']
_OUTS = [((KT, P, T), 'float32')]


def laid_out(inputs):
    import numpy as np

    a = {n: np.asarray(v) for n, v in inputs.items()}

    def block(w, c0, n):
        return w[:, c0:c0 + n].reshape(-1, P, n).transpose(1, 0, 2).reshape(P, -1)

    def column_blocks(w):
        return np.stack([block(w, c, BW) for c in range(0, w.shape[1], BW)])

    return {
        'x_t': np.ascontiguousarray(a['x'][0].T).reshape(KT, P, T),
        'p_t': np.ascontiguousarray(a['p'][0, 0].T).reshape(PLE // P, P, T),
        'gains_in': np.concatenate([a[n].reshape(-1, P).T for n in
                                    ('ln_mix', 'ln_ffn', 'ln_ple', 'ln_final', 'pool_scale', 'gla_norm')], axis=1),
        'w_in': np.concatenate([block(a['w_in'][0], c0, tiles * P) for c0, tiles, _ in BLOCKS_IN], axis=1),
        'w_gate_lr': a['w_gate_lr'], 'b_gate': a['b_gate'], 'w_pool': a['w_pool'],
        'w_out': column_blocks(a['w_out'][0]),
        'w_ffn_gate': column_blocks(a['w_ffn_gate'][0]),
        'w_ffn_up': column_blocks(a['w_ffn_up'][0]),
        'w_ffn_down': a['w_ffn_down'][0].reshape(GROUPS, BT, P, D).transpose(0, 2, 1, 3).reshape(GROUPS, P, BT * D),
        'w_ple_gate': column_blocks(a['w_ple_gate'][0]),
        'w_ple_proj': column_blocks(a['w_ple_proj'][0]),
        'consts': const_rows(),
    }


def kernel(**inputs):
    import numpy as _np
    import concourse.bacc as _bacc
    from concourse import mybir as _mybir
    from concourse.bass_utils import run_bass_kernel_spmd as _run

    nc = _bacc.Bacc("TRN2", target_bir_lowering=False, num_devices=1, dynamic_dma_scratch_size=1024)
    arrays, args = {}, []
    given = laid_out(inputs)
    for name in _INS:
        a = _np.ascontiguousarray(given[name])
        arrays[f"in_{name}_dram"] = a
        args.append(nc.dram_tensor(f"in_{name}_dram", a.shape, _mybir.dt.from_np(a.dtype), kind="ExternalInput").ap())
    for i, (shape, dtype) in enumerate(_OUTS):
        dt = _mybir.dt.from_np(_np.dtype(dtype))
        args.append(nc.dram_tensor(f"out_{i}_dram", shape, dt, kind="ExternalOutput").ap())
    hybrid_block(nc, *args)
    r = _run(nc, [arrays], core_ids=[0])
    got = tuple(r.results[0][f"out_{i}_dram"] for i in range(len(_OUTS)))
    return _np.ascontiguousarray(got[0].reshape(D, T).T).reshape(1, T, D)
```

```python
from contextlib import ExitStack

import concourse.bass as bass
from concourse import mybir

F32 = mybir.dt.float32
F32R = mybir.dt.float32r
U32 = mybir.dt.uint32
ALU = mybir.AluOpType
ACT = mybir.ActivationFunctionType

P = 128
T = 1024
D = 1024
KT = D // P
TC = 512
NC = T // TC
C = 128
NCH = T // C
HEADS, DK, DV = 4, 64, 128
KEY, VAL = HEADS * DK, HEADS * DV
KP = KEY // P
RANK = 16
PLE = 256
FF = 2816
BW = 256
BT = BW // P
WINDOWS = (2, 4, 8, 16)
NG = len(WINDOWS)
EPS = 1e-6
LEVELS = (64, 32, 16, 8, 4, 2, 1)
GROUPS = FF // BW
KB = 1024

OFF_V, OFF_G, OFF_LR = 2 * KEY, 2 * KEY + VAL, 2 * KEY + 2 * VAL
OFF_U = OFF_LR + RANK
Z_Q, Z_K, Z_V, Z_U, Z_G = 0, 2, 4, 8, 12
BLOCKS_IN = [(OFF_LR, 1), (KEY, 2), (0, 2), (OFF_U, 2), (OFF_U + BW, 2), (OFF_V, 2), (OFF_V + BW, 2), (OFF_G, 2),
             (OFF_G + BW, 2)]
NB = len(BLOCKS_IN)
BLOCK_AT = [sum(KT * P * tiles for _, tiles in BLOCKS_IN[:b]) for b in range(NB + 1)]
Z_OF = {2: Z_Q, 3: Z_U, 4: Z_U + 2, 7: Z_G, 8: Z_G + 2}

FILLS_AFTER = {(1, 3): [("gate", n) for n in range(4)], (2, 3): [("dec", n) for n in range(4)]}
for _j in range(4):
    FILLS_AFTER[3, _j] = [("diag", 2 * _j), ("diag", 2 * _j + 1)]
for _lev in range(len(LEVELS)):
    for _half in range(2):
        _at = (3 + (_lev + 1) // 2, 2 * ((_lev + 1) % 2) + _half)
        FILLS_AFTER[_at] = FILLS_AFTER.get(_at, []) + [(_lev, 2 * _half), (_lev, 2 * _half + 1)]
for _j in range(4):
    FILLS_AFTER[7, _j] = ([("kt", 2 * _j), ("kt", 2 * _j + 1)] if _j < 2 else [("kv", 2 * _j - 4), ("kv", 2 * _j - 3)]
                          ) + [("y", 2 * _j), ("y", 2 * _j + 1)]
FILLS_AFTER[8, 0] = [("o", 0), ("o", 1), ("o", 2)]
FILLS_AFTER[8, 1] = [("o", 3), ("o", 4), ("o", 5)]
FILLS_AFTER[8, 2] = [("o", 6), ("o", 7)]
FILLS_AFTER[8, 3] = [("ot", n) for n in range(8)]
NORM_FILLS = 2 * NC
FILL = {}
for _key in sorted(FILLS_AFTER):
    for _fill in FILLS_AFTER[_key]:
        FILL[_fill] = NORM_FILLS + len(FILL)
F_MIX_END = NORM_FILLS + len(FILL)


def const_rows():
    import numpy as np

    ident = np.eye(P, dtype=np.float32)
    tri = np.triu(np.ones((P, P), np.float32)) / 16.0
    masks = []
    for s in LEVELS:
        m = np.zeros((P, P // (2 * s), s), np.float32)
        for j in range(P):
            if j % (2 * s) < s:
                m[j, j // (2 * s), :] = 1.0
        masks.append(m.reshape(P, P // 2))
    inv = np.tile(1.0 / np.arange(1, 17, dtype=np.float32), (P, 1))
    return np.ascontiguousarray(np.concatenate([ident, tri] + masks + [inv], axis=1))


def hybrid_block(nc, x_t, p_t, gains_in, w_in, w_gate_lr, b_gate, w_pool, w_out, w_ffn_gate, w_ffn_up,
                 w_ffn_down, w_ple_gate, w_ple_proj, consts, out):
    ctx = ExitStack()
    with ctx:
        A0 = 2 * KB
        B0, H0, W0, S0 = A0 + 64 * KB, A0 + 128 * KB, A0 + 160 * KB, A0 + 208 * KB

        def at(name, shape, offset, dt=F32):
            return nc.alloc_sbuf_tensor_at(name, shape, dt, offset=offset)

        a_hi = at("a_hi", [P, KT, T], A0, F32R)
        a_lo = at("a_lo", [P, KT, T], A0 + 32 * KB, F32R)
        mix_hi = at("mix_hi", [P, KT, T], A0, F32R)
        mix_lo = at("mix_lo", [P, KT, T], A0 + 32 * KB, F32R)
        gu_hi = at("gu_hi", [P, BT, T], A0 + 24 * KB, F32R)
        gu_lo = at("gu_lo", [P, BT, T], A0 + 32 * KB, F32R)
        p_raw = at("p_raw", [P, PLE // P, T], A0 + 40 * KB)
        gate_t = at("gate_t", [P, 2, TC], A0 + 48 * KB)
        up_t = at("up_t", [P, 2, TC], A0 + 52 * KB)
        ple_t = at("ple_t", [P, 2, TC], A0 + 40 * KB)
        p_hi = at("p_hi", [P, PLE // P, T], A0 + 48 * KB, F32R)
        p_lo = at("p_lo", [P, PLE // P, T], A0 + 56 * KB, F32R)
        z = at("z", [P, 16, T], B0)
        pre = at("pre", [P, NCH, KEY], B0 + 48 * KB)
        soft = at("soft", [P, NCH, KEY], B0 + 56 * KB)
        decay = at("decay", [P, KP, T], B0 + 56 * KB)
        lr = at("lr", [RANK + 1, T], B0 + 16 * KB)
        tri = at("tri", [P, P], B0 + 20 * KB)
        w_gl = at("w_gl", [RANK + 1, KEY], B0 + 21 * KB)
        v_tok = at("v_tok", [P, NCH, VAL], B0 + 16 * KB)
        window = at("window", [P, 2, T], B0 + 48 * KB)
        gated = at("gated", [P, HEADS, T], B0)
        f_hi = at("f_hi", [P, KT, T], B0, F32R)
        f_lo = at("f_lo", [P, KT, T], B0 + 32 * KB, F32R)
        e_hi = at("e_hi", [P, KT, T], B0, F32R)
        e_lo = at("e_lo", [P, KT, T], B0 + 32 * KB, F32R)
        h = at("h", [P, KT, T], H0)
        scaled = at("scaled", [P, 2, KP * T], H0)
        attn = at("attn", [P, 2, NCH, KP, C], H0 + 16 * KB)
        state = at("state", [P, NCH, KP, DV], H0)
        k_tok = at("k_tok", [P, NCH, KEY], H0 + 8 * KB)
        o_tok = at("o_tok", [P, 2, NCH, KP, DV], H0 + 16 * KB)
        slot_at = [W0, W0 + 24 * KB, A0]
        w_raw = [at(f"w_raw{s}", [P, KT * BW], o) for s, o in enumerate(slot_at)]
        w_hi = [at(f"w_hi{s}", [P, KT * BW], o + 8 * KB, F32R) for s, o in enumerate(slot_at)]
        w_lo = [at(f"w_lo{s}", [P, KT * BW], o + 16 * KB, F32R) for s, o in enumerate(slot_at)]
        small = [S0]

        def sm(name, shape, dt=F32):
            t = at(name, shape, small[0], dt)
            n = 4
            for d in shape[1:]:
                n *= d
            small[0] += (n + 31) // 32 * 32
            return t

        rms_all = sm("rms_all", [P, T])
        sums = sm("sums", [P, T])
        ident = sm("ident", [P, P])
        masks = sm("masks", [P, len(LEVELS), P // 2])
        inv_t = sm("inv_t", [P, 16])
        ones = sm("ones", [P, P])
        w_pl_at = small[0]
        w_pl = sm("w_pl", [P, NG, P])
        head_t = sm("head_t", [P, 16])
        gains_all = sm("gains_all", [P, 4 * KT + NG + 1])
        gains = gains_all[:, 0:4 * KT].rearrange("p (n k) -> p n k", k=KT)
        g_pool, g_gla = gains_all[:, 4 * KT:4 * KT + NG], gains_all[:, 4 * KT + NG:4 * KT + NG + 1]
        stat = sm("stat", [P, 4, KT])
        o_stat = sm("o_stat", [P, 3, NCH * HEADS])
        o_sq = at("o_sq", [P, 2, TC], S0 + 4 * KB)
        last = sm("last", [P, KP, NCH])
        assert small[0] <= nc.sbuf_usable_end, small[0]
        squares = at("squares", [P, TC], w_pl_at)

        pb = [ctx.enter_context(nc.psum_tensor(f"pb{i}", [P, TC], F32)) for i in range(8)]

        def sem(name):
            return ctx.enter_context(nc.semaphore(name))

        class Ring:

            def __init__(self, name, first):
                self.filled, self.drained, self.first = sem(name + "_filled"), sem(name + "_drained"), first

            def bank(self, n):
                return pb[self.first + n % 4]

            def claim(self, n):
                if not isinstance(n, int) or n >= 4:
                    nc.tensor.wait_ge(self.drained, n - 3)

        def u_in(b):
            return 6 + 4 * (b - 2)

        U_OUT = u_in(NB)
        U_FFN = U_OUT + 16
        U_PLE = U_FFN + 8 * GROUPS
        F_NORM1, F_NORM2 = 0, F_MIX_END
        F_DOWN = F_NORM2 + NORM_FILLS
        F_NORM3 = F_DOWN + 16 * GROUPS
        F_NORM4 = F_NORM3 + NORM_FILLS
        proj, aux = Ring("proj", 0), Ring("aux", 4)

        w_landed = [sem(f"w_landed{s}") for s in range(3)]
        w_hi_ready = [sem(f"w_hi_ready{s}") for s in range(3)]
        w_lo_ready = [sem(f"w_lo_ready{s}") for s in range(3)]
        x_landed = [sem(f"x_landed{n}") for n in range(16)]
        small_landed, ident_landed, gate_w_landed, w_pool_landed, p_landed = (
            sem("small_landed"), sem("ident_landed"), sem("gate_w_landed"), sem("w_pool_landed"), sem("p_landed"))
        x_back, out_stored = sem("x_back"), sem("out_stored")
        ones_ready, lr_ones = sem("ones_ready"), sem("lr_ones")
        x_hi_done, x_lo_done, x_sq, x_sum = sem("x_hi_done"), sem("x_lo_done"), sem("x_sq"), sem("x_sum")
        root_ready, recip_ready, diag_ready = sem("root_ready"), sem("recip_ready"), sem("diag_ready")
        soft_ready, log_ready, last_ready = sem("soft_ready"), sem("log_ready"), sem("last_ready")
        diff_ready, exp_ready, scaled_ready, exp_b_ready, q_ready = (
            sem("diff_ready"), sem("exp_ready"), sem("scaled_ready"), sem("exp_b_ready"), sem("q_ready"))
        kv_step, silu_ready = sem("kv_step"), sem("silu_ready")
        window_step, window_ready, pooled_ready = sem("window_step"), sem("window_ready"), sem("pooled_ready")
        y_hi, y_lo = sem("y_hi"), sem("y_lo")
        o_squared, o_var, o_root, o_recip, o_scaled, o_hi, o_lo = (
            sem("o_squared"), sem("o_var"), sem("o_root"), sem("o_recip"), sem("o_scaled"), sem("o_hi"), sem("o_lo"))
        f_hi_done, f_lo_done, f_sq, f_sum = sem("f_hi_done"), sem("f_lo_done"), sem("f_sq"), sem("f_sum")
        gate_silu, gu_ready, gu_hi_ready, gu_lo_ready = (
            sem("gate_silu"), sem("gu_ready"), sem("gu_hi_ready"), sem("gu_lo_ready"))
        e_hi_done, e_lo_done, e_sq, e_sum = sem("e_hi_done"), sem("e_lo_done"), sem("e_sq"), sem("e_sum")
        p_hi_done, p_lo_done, ple_sig, h_final, y_sq, y_sum, y_normed = (
            sem("p_hi_done"), sem("p_lo_done"), sem("ple_sig"), sem("h_final"), sem("y_sq"), sem("y_sum"), sem("y_normed"))

        block = ctx.enter_context(nc.Block())

        def both(c):
            return slice(c * TC, (c + 1) * TC)

        def slot_of(b):
            return b % 2, b // 2

        S_GATE, S_UP, S_DOWN = 1, 0, 2
        FFN_USE = {S_UP: 7, S_GATE: 6, S_DOWN: 0}
        assert (NB + 4) // 2 == 6 and (NB + 5) // 2 == 7

        def ple_slot(b):
            s = (S_GATE, S_UP)[b % 2]
            return s, FFN_USE[s] + GROUPS + b // 2

        @block.sync
        def _(sp):
            def load(s, n, dst, src):
                if not (isinstance(n, int) and n == 0):
                    sp.wait_ge(w_lo_ready[s], n)
                sp.dma_start(dst, src).then_inc(w_landed[s], 16)

            def block_load(b):
                s, n = slot_of(b)
                if b < NB:
                    size = KT * P * BLOCKS_IN[b][1]
                    load(s, n, w_raw[s][:, 0:size], w_in[:, BLOCK_AT[b]:BLOCK_AT[b] + size])
                else:
                    load(s, n, w_raw[s][:], w_out[b - NB])

            sp.dma_start(gains_all[:], gains_in).then_inc(small_landed, 16)
            for n in range(16):
                k, c = n % KT, n // KT
                sp.dma_start(h[:, k, both(c)], x_t[k][:, both(c)]).then_inc(x_landed[n], 16)
                if n == 1:
                    block_load(0)
                if n == 7:
                    block_load(1)
                    sp.dma_start(ident[:], consts[:, 0:P]).then_inc(ident_landed, 16)
            block_load(2)
            sp.dma_start(tri[:], consts[:, P:2 * P]).then_inc(gate_w_landed, 16)
            sp.dma_start(w_gl[0:RANK, :], w_gate_lr[0]).then_inc(gate_w_landed, 16)
            sp.dma_start(w_gl[RANK:RANK + 1, :], b_gate).then_inc(gate_w_landed, 16)
            nm = len(LEVELS) * P // 2
            sp.dma_start(masks[:], consts[:, 2 * P:2 * P + nm].rearrange("p (l n) -> p l n", n=P // 2)
                         ).then_inc(gate_w_landed, 16)
            sp.dma_start(inv_t[:], consts[:, 2 * P + nm:]).then_inc(gate_w_landed, 16)
            sp.wait_ge(x_sum, 16)
            sp.dma_start(w_pl[:], w_pool[0].rearrange("g c d -> c g d")).then_inc(w_pool_landed, 16)
            for b in range(3, NB + 2):
                block_load(b)
            sp.wait_ge(o_scaled, 8)
            sp.wait_ge(aux.filled, F_MIX_END)
            for k in range(KT):
                sp.dma_start(h[:, k, :], x_t[k]).then_inc(x_back, 16)
            for b in range(NB + 2, NB + 4):
                block_load(b)

            def ffn_in(i):
                load(S_GATE, FFN_USE[S_GATE] + i, w_raw[S_GATE][:], w_ffn_gate[bass.ds(i, 1)].rearrange("g p n -> p (g n)"))
                load(S_UP, FFN_USE[S_UP] + i, w_raw[S_UP][:], w_ffn_up[bass.ds(i, 1)].rearrange("g p n -> p (g n)"))

            def ffn_down(i):
                load(S_DOWN, i, w_raw[S_DOWN][:], w_ffn_down[bass.ds(i, 1)].rearrange("g p n -> p (g n)"))

            ffn_in(0)
            sp.wait_ge(proj.filled, U_FFN)
            sp.dma_start(p_raw[:], p_t.rearrange("k p t -> p k t")).then_inc(p_landed, 16)
            ffn_down(0)
            with sp.Fori(0, GROUPS - 1) as i:
                ffn_in(i + 1)
                ffn_down(i + 1)
            for b in range(4):
                s, n = ple_slot(b)
                load(s, n, w_raw[s][:], w_ple_gate[b])
                load(2, GROUPS + b, w_raw[2][:, 0:2 * BW], w_ple_proj[b])
            for k in range(KT):
                sp.wait_ge(y_normed, 2 * (k + 1))
                sp.dma_start(out[k], h[:, k, :]).then_inc(out_stored, 16)
            sp.wait_ge(out_stored, 16 * KT)

        @block.gpsimd
        def _(pool):
            def lo_half(s, n, size):
                pool.wait_ge(w_hi_ready[s], n + 1)
                nc.gpsimd.tensor_tensor(w_lo[s][:, 0:size], w_raw[s][:, 0:size], w_hi[s][:, 0:size].bitcast(F32),
                                        ALU.subtract).then_inc(w_lo_ready[s], 1)

            nc.gpsimd.memset(ones[:], 1.0).then_inc(ones_ready, 1)
            nc.gpsimd.memset(lr[:], 1.0).then_inc(lr_ones, 1)
            steps = [0]

            def joined():
                pool.wait_ge(window_step, steps[0])

            def windowed(g):
                pool.wait_ge(proj.drained, u_in(3) + 2 * (g + 1))
                if g:
                    pool.wait_ge(pooled_ready, 2 * g)
                src = z[:, Z_U + g, :]
                for d in range(g + 1):
                    sh, dst = 1 << d, window[:, (d + g * 1 - g) % 2, :]
                    if d:
                        joined()
                    nc.gpsimd.tensor_tensor(dst[:, sh:T], src[:, sh:T], src[:, 0:T - sh], ALU.add).then_inc(window_step, 1)
                    nc.gpsimd.tensor_copy(dst[:, 0:sh], src[:, 0:sh]).then_inc(window_step, 1)
                    steps[0] += 2
                    src = dst
                joined()
                w = WINDOWS[g]
                nc.gpsimd.tensor_tensor(head_t[:, 0:w], src[:, 0:w], inv_t[:, 0:w], ALU.mult).then_inc(window_ready, 1)

            def block_lo(b):
                s, n = slot_of(b)
                lo_half(s, n, KT * (P * BLOCKS_IN[b][1] if b < NB else BW))

            for b in range(6):
                block_lo(b)
            pool.wait_ge(gate_w_landed, 16 * 5)
            windowed(0)
            windowed(1)
            block_lo(6)
            windowed(2)
            block_lo(7)
            windowed(3)
            block_lo(8)
            for c in range(NC):
                pool.wait_ge(y_hi, c + 1)
                nc.gpsimd.tensor_tensor(mix_lo[:, HEADS:KT, both(c)], z[:, Z_U:Z_U + NG, both(c)],
                                        mix_hi[:, HEADS:KT, both(c)].bitcast(F32), ALU.subtract).then_inc(y_lo, 1)
                block_lo(NB + c)
            for b in range(NB + 2, NB + 4):
                block_lo(b)
            with pool.Fori(0, GROUPS) as i:
                for s in (S_GATE, S_UP, S_DOWN):
                    lo_half(s, FFN_USE[s] + i, KT * BW)
            for b in range(4):
                lo_half(*ple_slot(b), KT * BW)
                lo_half(2, GROUPS + b, 2 * BW)

        @block.scalar
        def _(act):
            def hi_weights(s, n, size, used=None):
                act.wait_ge(w_landed[s], n * 16 + 16)
                if used is not None:
                    act.wait_ge(*used)
                nc.scalar.copy(w_hi[s][:, 0:size], w_raw[s][:, 0:size]).then_inc(w_hi_ready[s], 1)

            def block_hi(b):
                s, n = slot_of(b)
                used = None
                if b >= 2:
                    used = (proj.filled, {2: 4, 3: 6}.get(b, u_in(b - 1) if b < NB + 2 else U_OUT + 4 * (b - NB - 1)))
                hi_weights(s, n, KT * (P * BLOCKS_IN[b][1] if b < NB else BW), used)

            def root(norm, c):
                act.wait_ge(aux.drained, (F_NORM1, F_NORM2, F_NORM3, F_NORM4)[norm] + 2 * c + 1)
                nc.scalar.activation(stat[:, 1, 4 * c:4 * c + 4], stat[:, 0, 4 * c:4 * c + 4], ACT.Sqrt
                                     ).then_inc(root_ready, 1)

            def feed(n, m, c, ready, gain, hi, hi_sem, sq_sem, sum_sem):
                act.wait_ge(*ready)
                if gain is not None:
                    nc.scalar.activation(hi[:, m, both(c)], h[:, m, both(c)], ACT.Copy,
                                         scale=gains[:, gain, m:m + 1]).then_inc(hi_sem, 1)
                if n:
                    act.wait_ge(sum_sem, n)
                nc.scalar.activation(squares[:], h[:, m, both(c)], ACT.Square).then_inc(sq_sem, 1)

            act.wait_ge(small_landed, 16)
            for n in range(16):
                if n == 2:
                    block_hi(0)
                if n == 8:
                    block_hi(1)
                if n == 12:
                    root(0, 0)
                feed(n, n % KT, n // KT, (x_landed[n], 16), 0, a_hi, x_hi_done, x_sq, x_sum)
            root(0, 1)
            block_hi(2)
            act.wait_ge(aux.drained, FILL["gate", 3] + 1)
            nc.scalar.activation(soft[:], pre[:], ACT.Abs).then_inc(soft_ready, 1)
            act.wait_ge(soft_ready, 1)
            nc.scalar.activation(soft[:], soft[:], ACT.Exp, scale=-1.0).then_inc(soft_ready, 1)
            act.wait_ge(soft_ready, 2)
            nc.scalar.activation(soft[:], soft[:], ACT.Ln, bias=1.0).then_inc(soft_ready, 1)
            block_hi(3)

            def exp_diff(lev):
                act.wait_ge(diff_ready, 2 * (lev + 1) if lev < len(LEVELS) else 2 * len(LEVELS) + 1)
                nc.scalar.activation(scaled[:, lev % 2, :], scaled[:, lev % 2, :], ACT.Exp).then_inc(exp_ready, 1)

            exp_diff(0)
            act.wait_ge(aux.drained, FILL["dec", 3] + 1)
            nc.scalar.activation(last[:], decay[:].rearrange("p a (t c) -> p a t c", c=C)[:, :, :, C - 1], ACT.Exp
                                 ).then_inc(last_ready, 1)
            exp_diff(1)
            for b in range(4, 8):
                block_hi(b)
                exp_diff(2 * b - 6) if b < 7 else None
                exp_diff(2 * b - 5) if b < 7 else None
            act.wait_ge(aux.filled, FILL[len(LEVELS) - 1, 3] + 1)
            nc.scalar.activation(scaled[:, 0, :], decay[:].rearrange("p a t -> p (a t)"), ACT.Exp).then_inc(exp_b_ready, 1)

            def silu_unit(b, j):
                act.wait_ge(proj.drained, u_in(b) + j + 1)
                g = z[:, Z_OF[b] + j // 2, both(j % 2)]
                nc.scalar.activation(g, g, ACT.Silu).then_inc(silu_ready, 1)

            def square_o(f):
                act.wait_ge(aux.drained, FILL["o", f] + 1)
                if f >= 2:
                    act.wait_ge(o_squared, f - 1)
                for q in range(4):
                    i = nc.scalar.activation(o_sq[:, f % 2, q * DV:(q + 1) * DV],
                                             o_tok[:, f % 2, 2 * (f // 2) + q // 2, q % 2, :], ACT.Square,
                                             accum_out=o_stat[:, 0, 4 * f + q:4 * f + q + 1])
                i.then_inc(o_squared, 1)

            for j in range(4):
                silu_unit(7, j)
                if j == 0:
                    block_hi(8)
            for f in range(3):
                square_o(f)
            silu_unit(8, 0)
            for f in range(3, 6):
                square_o(f)
            silu_unit(8, 1)
            for f in range(6, 8):
                square_o(f)
            silu_unit(8, 2)
            act.wait_ge(o_var, 1)
            nc.scalar.activation(o_stat[:, 2, :], o_stat[:, 1, :], ACT.Sqrt).then_inc(o_root, 1)
            block_hi(NB)
            act.wait_ge(proj.filled, U_OUT)
            for c in range(NC):
                act.wait_ge(aux.drained, FILL["y", 7] + 1)
                nc.scalar.copy(mix_hi[:, HEADS:KT, both(c)], z[:, Z_U:Z_U + NG, both(c)]).then_inc(y_hi, 1)
                if c == 0:
                    silu_unit(8, 3)
                for hd in range(HEADS):
                    act.wait_ge(aux.drained, FILL["ot", 4 * c + hd] + 1)
                    nc.scalar.copy(mix_hi[:, hd, both(c)], gated[:, hd, both(c)]).then_inc(o_hi, 1)
            block_hi(NB + 1)

            for n in range(16):
                if n in (4, 8):
                    block_hi(NB + 1 + n // 4)
                if n == 12:
                    hi_weights(S_GATE, FFN_USE[S_GATE], KT * BW, (proj.filled, U_OUT + 12))
                feed(n, n // NC, n % NC, (proj.drained, U_OUT + n + 1), 1, f_hi, f_hi_done, f_sq, f_sum)
            hi_weights(S_UP, FFN_USE[S_UP], KT * BW, (proj.filled, U_FFN))
            root(1, 0)
            root(1, 1)
            hi_weights(S_DOWN, 0, KT * BW)

            def ffn_pair(i, n):
                act.wait_ge(proj.drained, i * 8 + (U_FFN + 2 * n + 1))
                nc.scalar.activation(gate_t[:, n % 2, :], gate_t[:, n % 2, :], ACT.Silu).then_inc(gate_silu, 1)
                act.wait_ge(gu_ready, i * 4 + (n + 1))
                nc.scalar.copy(gu_hi[:, n // 2, both(n % 2)], up_t[:, n % 2, :]).then_inc(gu_hi_ready, 1)

            with act.Fori(0, GROUPS - 1) as i:
                for n in range(4):
                    ffn_pair(i, n)
                hi_weights(S_GATE, i + (FFN_USE[S_GATE] + 1), KT * BW, (proj.filled, i * 8 + (U_FFN + 7)))
                hi_weights(S_UP, i + (FFN_USE[S_UP] + 1), KT * BW, (proj.filled, i * 8 + (U_FFN + 8)))
                hi_weights(S_DOWN, i + 1, KT * BW, (aux.filled, i * 16 + (F_DOWN + 16)))
            for n in range(4):
                ffn_pair(GROUPS - 1, n)
            hi_weights(*ple_slot(0), KT * BW, (proj.filled, U_PLE - 1))
            hi_weights(*ple_slot(1), KT * BW, (proj.filled, U_PLE))
            for n in range(16):
                feed(n, n % KT, n // KT, (aux.drained, F_NORM3 - 16 + n + 1), 2, e_hi, e_hi_done, e_sq, e_sum)
                if n == 3:
                    act.wait_ge(p_landed, 16)
                    for k in range(PLE // P):
                        nc.scalar.copy(p_hi[:, k, :], p_raw[:, k, :]).then_inc(p_hi_done, 1)
            hi_weights(2, GROUPS, 2 * BW, (aux.filled, F_NORM3))
            root(2, 0)
            root(2, 1)
            for n in range(16):
                b = n // 4
                if n % 4 == 0 and b > 0:
                    hi_weights(2, GROUPS + b, 2 * BW, (proj.filled, U_PLE + 8 * b))
                    if b < 3:
                        hi_weights(*ple_slot(b + 1), KT * BW, (proj.filled, U_PLE + 8 * b - 1))
                act.wait_ge(proj.drained, U_PLE + 2 * n + 1)
                nc.scalar.activation(ple_t[:, n % 2, :], ple_t[:, n % 2, :], ACT.Sigmoid).then_inc(ple_sig, 1)
                feed(n, n // NC, n % NC, (h_final, n + 1), None, None, None, y_sq, y_sum)
            root(3, 0)
            root(3, 1)

        @block.vector
        def _(dve):
            V = nc.vector

            def norm_var(f0, c):
                dve.wait_ge(aux.filled, f0 + 2 * c + 1)
                V.tensor_scalar(stat[:, 0, 4 * c:4 * c + 4], aux.bank(f0 + 2 * c)[:, 0:4], 1.0 / D, EPS, ALU.mult, ALU.add
                                ).then_inc(aux.drained, 1)

            def norm_diag(norm, c):
                dve.wait_ge(root_ready, 2 * norm + c + 1)
                r = stat[:, 3, 4 * c:4 * c + 4]
                V.reciprocal(r, stat[:, 1, 4 * c:4 * c + 4]).then_inc(recip_ready, 1)
                dve.wait_ge(recip_ready, 2 * norm + c + 1)
                V.tensor_tensor(sums[:, both(c)].rearrange("p (t c) -> p t c", c=P),
                                ident[:].unsqueeze(1).broadcast_to([P, 4, P]),
                                r.unsqueeze(2).broadcast_to([P, 4, P]), ALU.mult).then_inc(diag_ready, 1)

            def norm_take(f0, c):
                f = f0 + 2 * c + 1
                dve.wait_ge(aux.filled, f + 1)
                V.tensor_copy(rms_all[:, both(c)], aux.bank(f)[:]).then_inc(aux.drained, 1)

            def norm_stats(f0, norm):
                for c in range(NC):
                    norm_var(f0, c)
                    norm_diag(norm, c)
                    norm_take(f0, c)
                dve.wait_ge(aux.drained, f0 + NORM_FILLS)

            def feed(n, m, c, gain, hi, lo, hi_sem, lo_sem, sq_sem, sum_sem):
                if gain is not None:
                    dve.wait_ge(hi_sem, n + 1)
                    V.scalar_tensor_tensor(out=lo[:, m, both(c)], in0=h[:, m, both(c)], scalar=gains[:, gain, m:m + 1],
                                           in1=hi[:, m, both(c)].bitcast(F32), op0=ALU.mult,
                                           op1=ALU.subtract).then_inc(lo_sem, 1)
                dve.wait_ge(sq_sem, n + 1)
                if m == 0:
                    V.tensor_copy(sums[:, both(c)], squares[:]).then_inc(sum_sem, 1)
                else:
                    dve.wait_ge(sum_sem, n)
                    V.tensor_tensor(sums[:, both(c)], sums[:, both(c)], squares[:], ALU.add).then_inc(sum_sem, 1)

            dve.wait_ge(small_landed, 16)
            for n in range(16):
                if n == 10:
                    norm_var(F_NORM1, 0)
                if n == 13:
                    dve.wait_ge(ident_landed, 16)
                    norm_diag(0, 0)
                dve.wait_ge(x_landed[n], 16)
                feed(n, n % KT, n // KT, 0, a_hi, a_lo, x_hi_done, x_lo_done, x_sq, x_sum)
            norm_take(F_NORM1, 0)
            dve.wait_ge(aux.drained, F_NORM1 + 2)
            dve.wait_ge(lr_ones, 1)

            def lr_unit(u, c):
                dve.wait_ge(proj.filled, u + 1)
                V.tensor_tensor(lr[0:RANK, both(c)], proj.bank(u)[0:RANK, :], rms_all[0:RANK, both(c)], ALU.mult
                                ).then_inc(proj.drained, 1)

            def tile_unit(u, n, c):
                dve.wait_ge(proj.filled, u + 1)
                V.tensor_tensor(z[:, n, both(c)], proj.bank(u)[:], rms_all[:, both(c)], ALU.mult
                                ).then_inc(proj.drained, 1)

            def v_unit(b, j):
                u = u_in(b) + j
                dve.wait_ge(proj.filled, u + 1)
                V.tensor_tensor(v_tok[:, 2 * j:2 * j + 2, (b - 5) * BW:(b - 4) * BW],
                                proj.bank(u)[:].rearrange("p (t n) -> p t n", t=2),
                                stat[:, 3, 2 * j:2 * j + 2].unsqueeze(2).broadcast_to([P, 2, BW]), ALU.mult
                                ).then_inc(proj.drained, 1)

            lr_unit(0, 0)
            tile_unit(1, Z_K, 0)
            tile_unit(2, Z_K + 1, 0)
            norm_var(F_NORM1, 1)
            norm_diag(0, 1)
            norm_take(F_NORM1, 1)
            dve.wait_ge(aux.drained, F_NORM1 + 4)
            lr_unit(3, 1)
            tile_unit(4, Z_K, 1)
            tile_unit(5, Z_K + 1, 1)

            flat_b = decay[:].rearrange("p a t -> p (a t)")
            flat_k = z[:, Z_K:Z_K + KP, :].rearrange("p a t -> p (a t)")
            flat_q = z[:, Z_Q:Z_Q + KP, :].rearrange("p a t -> p (a t)")

            def halves(ap, s):
                v = ap.rearrange("p (n s) -> p n s", s=2 * s)
                return v[:, :, 0:s], v[:, :, s:2 * s]

            def level_diff(lev):
                s = LEVELS[lev]
                left, right = halves(flat_b, s)
                ref = flat_b.rearrange("p (n s) -> p n s", s=2 * s)[:, :, s - 1:s].broadcast_to([P, KP * T // (2 * s), s])
                o_left, o_right = halves(scaled[:, lev % 2, :], s)
                V.tensor_tensor(o_left, ref, left, ALU.subtract).then_inc(diff_ready, 1)
                V.tensor_tensor(o_right, right, ref, ALU.subtract).then_inc(diff_ready, 1)

            def level_scale(lev):
                s = LEVELS[lev]
                dve.wait_ge(exp_ready, lev + 1)
                o_left, o_right = halves(scaled[:, lev % 2, :], s)
                V.tensor_tensor(o_left, o_left, halves(flat_k, s)[0], ALU.mult).then_inc(scaled_ready, 1)
                V.scalar_tensor_tensor(out=o_right, in0=halves(flat_q, s)[1], scalar=DK ** -0.5, in1=o_right,
                                       op0=ALU.mult, op1=ALU.mult).then_inc(scaled_ready, 1)

            def k_diff():
                b4 = decay[:].rearrange("p a (t c) -> p (a t) c", c=C)
                V.tensor_tensor(scaled[:, 1, :].rearrange("p (n c) -> p n c", c=C),
                                b4[:, :, C - 1:C].broadcast_to([P, KP * NCH, C]), b4, ALU.subtract
                                ).then_inc(diff_ready, 1)

            def k_scale():
                dve.wait_ge(exp_ready, len(LEVELS) + 1)
                V.tensor_tensor(flat_k, flat_k, scaled[:, 1, :], ALU.mult).then_inc(scaled_ready, 1)

            kv_steps = [0]

            def drain(kind, n):
                f = FILL[kind, n]
                dve.wait_ge(aux.filled, f + 1)
                bank = aux.bank(f)[:]
                if kind == "gate":
                    i = V.tensor_copy(pre[:, 2 * n:2 * n + 2, :], bank.rearrange("p (t n) -> p t n", t=2))
                elif kind == "dec":
                    if n == 0:
                        dve.wait_ge(aux.filled, f + 4)
                    i = V.tensor_copy(decay[:, n // 2, both(n % 2)], bank)
                elif kind == "diag":
                    r, t2 = n % 2, n // 2
                    i = V.scalar_tensor_tensor(
                        out=attn[:, r, 2 * t2:2 * t2 + 2, :, :].rearrange("p t a c -> p (t a) c"),
                        in0=bank.rearrange("p (a c) -> p a c", c=C), scalar=DK ** -0.5,
                        in1=ident[:].unsqueeze(1).broadcast_to([P, 2 * KP, C]), op0=ALU.mult, op1=ALU.mult)
                elif kind == "kt":
                    i = V.tensor_copy(k_tok[:, 2 * n:2 * n + 2, :], bank.rearrange("p (t c) -> p t c", t=2))
                elif kind == "y":
                    g, c = n // NC, n % NC
                    i = V.tensor_scalar(z[:, Z_U + g, both(c)], bank, g_pool[:, g:g + 1], None, ALU.mult)
                elif kind == "kv":
                    for t in range(2 * n, min(2 * n + 2, NCH - 1)):
                        part = bank[:, (t % 2) * 2 * DV:(t % 2 + 1) * 2 * DV].rearrange("p (a v) -> p a v", a=KP)
                        closing = t == min(2 * n + 1, NCH - 2)
                        if t == 0:
                            V.tensor_copy(state[:, 1, :, :], part).then_inc(kv_step, 1)
                            kv_steps[0] += 1
                            continue
                        dve.wait_ge(kv_step, kv_steps[0])
                        if t == 2 * n:
                            dve.wait_ge(aux.drained, f)
                        for a in range(KP):
                            i = V.scalar_tensor_tensor(
                                out=state[:, t + 1, a, :], in0=state[:, t, a, :], scalar=last[:, a, t:t + 1],
                                in1=part[:, a, :], op0=ALU.mult, op1=ALU.add)
                            if not (closing and a == KP - 1):
                                i.then_inc(kv_step, 1)
                                kv_steps[0] += 1
                elif kind == "o":
                    i = V.tensor_copy(o_tok[:, n % 2, 2 * (n // 2):2 * (n // 2) + 2, :, :].rearrange("p t a c -> p (t a) c"),
                                      bank.rearrange("p (q c) -> p q c", c=DV))
                elif kind == "ot":
                    c, hd = n // HEADS, n % HEADS
                    i = V.scalar_tensor_tensor(out=gated[:, hd, both(c)], in0=bank, scalar=g_gla,
                                               in1=z[:, Z_G + hd, both(c)], op0=ALU.mult, op1=ALU.mult)
                else:
                    s, r, c = LEVELS[kind], n % 2, n // 2
                    dst = attn[:, r, 4 * c:4 * c + 4, :, :].rearrange("p t a (n s) -> p (t a) n s", s=2 * s)[:, :, :, s:2 * s]
                    m = masks[:, kind, :].rearrange("p (n s) -> p n s", s=s).unsqueeze(1).broadcast_to(
                        [P, 4 * KP, C // (2 * s), s])
                    before = FILL["diag", 4 * c + r + 2] if kind == 0 else FILL[kind - 1, n]
                    dve.wait_ge(aux.drained, before + 1)
                    i = V.copy_predicated(dst, m.bitcast(U32), bank.rearrange("p (a n s) -> p a n s", a=4 * KP, s=s))
                i.then_inc(aux.drained, 1)

            def drains_after(b, j):
                for kind, n in FILLS_AFTER.get((b, j), []):
                    drain(kind, n)

            def pooled(g):
                w = WINDOWS[g]
                dve.wait_ge(window_ready, g + 1)
                V.scalar_tensor_tensor(out=z[:, Z_U + g, w:T], in0=window[:, g % 2, w:T], scalar=1.0 / w,
                                       in1=z[:, Z_U + g, w:T], op0=ALU.mult, op1=ALU.subtract).then_inc(pooled_ready, 1)
                V.tensor_tensor(z[:, Z_U + g, 0:w], head_t[:, 0:w], z[:, Z_U + g, 0:w], ALU.subtract
                                ).then_inc(pooled_ready, 1)

            dve.wait_ge(gate_w_landed, 16 * 5)
            drains_after(1, 3)
            for j in range(4):
                tile_unit(u_in(2) + j, Z_Q + j // 2, j % 2)
                if j == 1:
                    dve.wait_ge(soft_ready, 3)
                    V.scalar_tensor_tensor(out=soft[:], in0=pre[:], scalar=0.0, in1=soft[:], op0=ALU.min,
                                           op1=ALU.subtract).then_inc(log_ready, 1)
            drains_after(2, 3)
            dve.wait_ge(aux.drained, FILL["dec", 3] + 1)
            dve.wait_ge(proj.drained, u_in(3))
            dve.wait_ge(x_lo_done, 16)
            level_diff(0)
            for b in range(3, NB):
                for j in range(4):
                    lev = 2 * (b - 3) + j // 2
                    if j % 2 == 0 and b < 7 and lev:
                        level_diff(lev) if lev < len(LEVELS) else k_diff()
                    if b == 8 and j == 0:
                        dve.wait_ge(last_ready, 1)
                    if b == 8 and j == 3:
                        dve.wait_ge(o_squared, 8)
                        V.tensor_scalar(o_stat[:, 1, :], o_stat[:, 0, :], 1.0 / DV, EPS, ALU.mult, ALU.add
                                        ).then_inc(o_var, 1)
                        dve.wait_ge(o_root, 1)
                        V.reciprocal(o_stat[:, 1, :], o_stat[:, 2, :]).then_inc(o_recip, 1)
                        dve.wait_ge(o_recip, 1)
                        for f in range(8):
                            ov = o_tok[:, f % 2, 2 * (f // 2):2 * (f // 2) + 2, :, :].rearrange("p t a c -> p (t a) c")
                            V.tensor_tensor(ov, ov, o_stat[:, 1, 4 * f:4 * f + 4].unsqueeze(2).broadcast_to([P, 4, DV]),
                                            ALU.mult).then_inc(o_scaled, 1)
                    if b in (5, 6):
                        v_unit(b, j)
                    else:
                        tile_unit(u_in(b) + j, Z_OF[b] + j // 2, j % 2)
                    if b == 8 and j == 3:
                        break
                    drains_after(b, j)
                    if j % 2 == 0 and b < 7:
                        level_scale(lev) if lev < len(LEVELS) else k_scale()
                    if (b, j) in ((5, 1), (5, 3), (6, 1), (6, 3)):
                        pooled(((5, 1), (5, 3), (6, 1), (6, 3)).index((b, j)))
                    if (b, j) == (7, 0):
                        dve.wait_ge(exp_b_ready, 1)
                        V.scalar_tensor_tensor(out=flat_q, in0=flat_q, scalar=DK ** -0.5, in1=scaled[:, 0, :],
                                               op0=ALU.mult, op1=ALU.mult).then_inc(q_ready, 1)
                        dve.wait_ge(q_ready, 1)

            def o_low(n):
                c, hd = n // HEADS, n % HEADS
                dve.wait_ge(o_hi, n + 1)
                V.tensor_tensor(mix_lo[:, hd, both(c)], gated[:, hd, both(c)], mix_hi[:, hd, both(c)].bitcast(F32),
                                ALU.subtract).then_inc(o_lo, 1)

            dve.wait_ge(silu_ready, 8)
            for n in range(8):
                drain("ot", n)
                if n:
                    o_low(n - 1)
            o_low(7)

            dve.wait_ge(x_back, 16 * KT)

            for n in range(16):
                m, c = n // NC, n % NC
                dve.wait_ge(proj.filled, U_OUT + n + 1)
                V.tensor_tensor(h[:, m, both(c)], h[:, m, both(c)], proj.bank(U_OUT + n)[:], ALU.add
                                ).then_inc(proj.drained, 1)
                if n:
                    feed(n - 1, (n - 1) // NC, (n - 1) % NC, 1, f_hi, f_lo, f_hi_done, f_lo_done, f_sq, f_sum)
            feed(15, KT - 1, 1, 1, f_hi, f_lo, f_hi_done, f_lo_done, f_sq, f_sum)
            norm_stats(F_NORM2, 1)

            def ffn_pair(i, n):
                c = n % 2
                dve.wait_ge(proj.filled, i * 8 + (U_FFN + 2 * n + 1))
                V.tensor_tensor(gate_t[:, c, :], proj.bank(U_FFN + 2 * n)[:], rms_all[:, both(c)], ALU.mult
                                ).then_inc(proj.drained, 1)
                dve.wait_ge(proj.filled, i * 8 + (U_FFN + 2 * n + 2))
                V.tensor_tensor(up_t[:, c, :], proj.bank(U_FFN + 2 * n + 1)[:], rms_all[:, both(c)], ALU.mult
                                ).then_inc(proj.drained, 1)
                dve.wait_ge(gate_silu, i * 4 + (n + 1))
                dve.wait_ge(proj.drained, i * 8 + (U_FFN + 2 * n + 2))
                V.tensor_tensor(up_t[:, c, :], gate_t[:, c, :], up_t[:, c, :], ALU.mult).then_inc(gu_ready, 1)
                dve.wait_ge(gu_hi_ready, i * 4 + (n + 1))
                V.tensor_tensor(gu_lo[:, n // 2, both(c)], up_t[:, c, :], gu_hi[:, n // 2, both(c)].bitcast(F32),
                                ALU.subtract).then_inc(gu_lo_ready, 1)

            def ffn_add(i, n):
                m, c = n % KT, n // KT
                dve.wait_ge(aux.filled, i * 16 + (F_DOWN + n + 1))
                V.tensor_tensor(h[:, m, both(c)], h[:, m, both(c)], aux.bank(F_DOWN + n)[:], ALU.add
                                ).then_inc(aux.drained, 1)

            with dve.Fori(0, GROUPS - 1) as i:
                for n in range(4):
                    ffn_pair(i, n)
                for n in range(16):
                    ffn_add(i, n)
            for n in range(4):
                ffn_pair(GROUPS - 1, n)
            for n in range(16):
                ffn_add(GROUPS - 1, n)
                if n:
                    feed(n - 1, (n - 1) % KT, (n - 1) // KT, 2, e_hi, e_lo, e_hi_done, e_lo_done, e_sq, e_sum)
            feed(15, KT - 1, 1, 2, e_hi, e_lo, e_hi_done, e_lo_done, e_sq, e_sum)
            for k in range(PLE // P):
                dve.wait_ge(p_hi_done, k + 1)
                V.tensor_tensor(p_lo[:, k, :], p_raw[:, k, :], p_hi[:, k, :].bitcast(F32), ALU.subtract
                                ).then_inc(p_lo_done, 1)
            norm_stats(F_NORM3, 2)

            for n in range(16):
                m, c = n // NC, n % NC
                u = U_PLE + 2 * n
                dve.wait_ge(proj.filled, u + 1)
                V.tensor_tensor(ple_t[:, n % 2, :], proj.bank(u)[:], rms_all[:, both(c)], ALU.mult
                                ).then_inc(proj.drained, 1)
                dve.wait_ge(proj.filled, u + 2)
                dve.wait_ge(ple_sig, n + 1)
                V.tensor_tensor(ple_t[:, n % 2, :], ple_t[:, n % 2, :], proj.bank(u + 1)[:], ALU.mult
                                ).then_inc(proj.drained, 1)
                dve.wait_ge(proj.drained, u + 2)
                V.tensor_tensor(h[:, m, both(c)], h[:, m, both(c)], ple_t[:, n % 2, :], ALU.add).then_inc(h_final, 1)
                if n:
                    feed(n - 1, (n - 1) // NC, (n - 1) % NC, None, None, None, None, None, y_sq, y_sum)
            feed(15, KT - 1, 1, None, None, None, None, None, y_sq, y_sum)
            norm_stats(F_NORM4, 3)
            for n in range(16):
                m, c = n // NC, n % NC
                V.scalar_tensor_tensor(out=h[:, m, both(c)], in0=h[:, m, both(c)], scalar=gains[:, 3, m:m + 1],
                                       in1=rms_all[:, both(c)], op0=ALU.mult, op1=ALU.mult).then_inc(y_normed, 1)

        @block.tensor
        def _(pe):
            M = nc.tensor.matmul

            def split3(bank, w_h, w_l, x_h, x_l, start, stop):
                M(bank, w_h, x_h, start=start, stop=False)
                M(bank, w_h, x_l, start=False, stop=False)
                return M(bank, w_l, x_h, start=False, stop=stop)

            def unit(n, s, tiles, m, x_h, x_l, c, kts=KT, ready=None):
                wh = w_hi[s][:, 0:kts * tiles * P].rearrange("p (k n) -> p k n", k=kts)
                wl = w_lo[s][:, 0:kts * tiles * P].rearrange("p (k n) -> p k n", k=kts)
                cols = slice(m * P, (m + 1) * P)
                for k in range(kts):
                    if ready is not None:
                        ready(k)
                    i = split3(proj.bank(n)[:], wh[:, k, cols], wl[:, k, cols], x_h[:, k, both(c)], x_l[:, k, both(c)],
                               k == 0, k == kts - 1)
                i.then_inc(proj.filled, 1)

            def v_unit(n, s, j):
                wh, wl = (w[s][:].rearrange("p (k n) -> p k n", k=KT) for w in (w_hi, w_lo))
                for t in (2 * j, 2 * j + 1):
                    bank, rows = proj.bank(n)[:, (t % 2) * BW:(t % 2 + 1) * BW], slice(t * C, (t + 1) * C)
                    for k in range(KT):
                        i = split3(bank, a_hi[:, k, rows], a_lo[:, k, rows], wh[:, k, :], wl[:, k, :], k == 0, k == KT - 1)
                i.then_inc(proj.filled, 1)

            def token_sums(f0, c, ready):
                pe.wait_ge(*ready)
                aux.claim(f0 + 2 * c)
                for t in range(4):
                    i = M(aux.bank(f0 + 2 * c)[:, t:t + 1], sums[:, (4 * c + t) * P:(4 * c + t + 1) * P], ones[:, 0:1],
                          start=True, stop=True)
                i.then_inc(aux.filled, 1)

            def spread_rms(f0, norm, c):
                pe.wait_ge(diag_ready, 2 * norm + c + 1)
                aux.claim(f0 + 2 * c + 1)
                M(aux.bank(f0 + 2 * c + 1)[:], ones[:], sums[:, both(c)], start=True, stop=True).then_inc(aux.filled, 1)

            def fill(kind, n):
                f = FILL[kind, n]
                r, c = n % 2, n // 2
                rows = slice(r * DK, (r + 1) * DK)
                if kind == "o" and n == 0:
                    pe.wait_ge(kv_step, 9)
                    pe.wait_ge(aux.drained, f)
                elif kind == "o" or kind in range(len(LEVELS)) and n:
                    pass
                elif kind == "gate" and n == 0:
                    pe.wait_ge(proj.drained, 4)
                    pe.wait_ge(gate_w_landed, 16 * 5)
                elif kind == "dec" and n == 0:
                    pe.wait_ge(log_ready, 1)
                elif kind == "diag" and n == 0:
                    pe.wait_ge(proj.drained, u_in(3))
                elif kind == "kt" and n == 0:
                    pe.wait_ge(scaled_ready, 2 * len(LEVELS) + 1)
                elif kind == "kv" and n == 0:
                    pe.wait_ge(aux.drained, FILL["kt", 3] + 1)
                elif kind == "y":
                    pe.wait_ge(pooled_ready, 2 * (n // NC) + 2)
                    pe.wait_ge(w_pool_landed, 16)
                elif kind == "ot":
                    pe.wait_ge(o_scaled, 8)
                elif n == 0:
                    pe.wait_ge(scaled_ready, 2 * (kind + 1))
                aux.claim(f)
                bank = aux.bank(f)
                if kind == "gate":
                    for j in range(2):
                        t = 2 * n + j
                        i = M(bank[:, j * KEY:(j + 1) * KEY], lr[:, t * C:(t + 1) * C], w_gl[:], start=True, stop=True)
                elif kind == "dec":
                    for j in range(4):
                        i = M(bank[:, j * C:(j + 1) * C], soft[:, 4 * (n % 2) + j, (n // 2) * P:(n // 2 + 1) * P], tri[:],
                              start=True, stop=True)
                elif kind == "diag":
                    for j in range(4):
                        t, a = 2 * c + j // 2, j % 2
                        i = M(bank[:, j * C:(j + 1) * C], z[rows, Z_K + a, t * C:(t + 1) * C],
                              z[rows, Z_Q + a, t * C:(t + 1) * C], start=True, stop=True)
                elif kind == "kt":
                    for j in range(4):
                        t, a = 2 * n + j // 2, j % 2
                        i = nc.tensor.transpose(bank[:, j * P:(j + 1) * P], z[:, Z_K + a, t * C:(t + 1) * C], ident[:])
                elif kind == "kv":
                    for t in range(2 * n, min(2 * n + 2, NCH - 1)):
                        for a in range(KP):
                            for half in range(2):
                                col = ((t % 2) * KP + a) * DV
                                i = M(bank[half * DK:(half + 1) * DK, col:col + DV],
                                      k_tok[:, t, a * P + half * DK:a * P + (half + 1) * DK],
                                      v_tok[:, t, (2 * a + half) * DV:(2 * a + half + 1) * DV], start=True, stop=True)
                elif kind == "y":
                    g, c = n // NC, n % NC
                    i = M(bank[:], w_pl[:, g, :], z[:, Z_U + g, both(c)], start=True, stop=True)
                elif kind == "o":
                    for q in range(4):
                        t, a = 2 * c + q // 2, q % 2
                        o = bank[:, q * DV:(q + 1) * DV]
                        if t:
                            M(o, z[rows, Z_Q + a, t * C:(t + 1) * C], state[rows, t, a, :], start=True, stop=False)
                        i = M(o, attn[:, r, t, a, :], v_tok[:, t, (2 * a + r) * DV:(2 * a + r + 1) * DV],
                              start=t == 0, stop=True)
                elif kind == "ot":
                    c, hd = n // HEADS, n % HEADS
                    for j in range(4):
                        i = nc.tensor.transpose(bank[:, j * P:(j + 1) * P], o_tok[:, hd % 2, 4 * c + j, hd // 2, :], ident[:])
                else:
                    s = LEVELS[kind]
                    sc = scaled[:, kind % 2, :].rearrange("p (a t c) -> p a t c", a=KP, c=C)
                    for j in range(4 * KP):
                        t, a = 4 * c + j // KP, j % KP
                        right = sc[rows, a, t, :].rearrange("p (n s) -> p n s", s=2 * s)[:, :, s:2 * s]
                        i = M(bank[:, j * C // 2:(j + 1) * C // 2], sc[rows, a, t, :], right, start=True, stop=True)
                i.then_inc(aux.filled, 1)

            def fills_after(b, j):
                for kind, n in FILLS_AFTER.get((b, j), []):
                    fill(kind, n)

            pe.wait_ge(w_lo_ready[0], 1)
            pe.wait_ge(ones_ready, 1)
            for c in range(NC):
                proj.claim(3 * c)
                unit(3 * c, 0, 1, 0, a_hi, a_lo, c, ready=lambda k: pe.wait_ge(x_lo_done, KT * c + k + 1))
                if c == 0:
                    pe.wait_ge(w_lo_ready[1], 1)
                token_sums(F_NORM1, c, (x_sum, 8 * (c + 1)))
                for m in range(2):
                    proj.claim(3 * c + 1 + m)
                    unit(3 * c + 1 + m, 1, 2, m, a_hi, a_lo, c)
                    if m == 0:
                        spread_rms(F_NORM1, 0, c)
            fills_after(1, 3)
            for b in range(2, NB):
                s, n = slot_of(b)
                pe.wait_ge(w_lo_ready[s], n + 1)
                for j in range(4):
                    u = u_in(b) + j
                    proj.claim(u)
                    if b in (5, 6):
                        v_unit(u, s, j)
                    else:
                        unit(u, s, 2, j // 2, a_hi, a_lo, j % 2)
                    fills_after(b, j)

            def mix_ready(c):
                return lambda k: pe.wait_ge(o_lo, HEADS * c + k + 1) if k < HEADS else pe.wait_ge(y_lo, c + 1)

            for b in range(4):
                s, n = slot_of(NB + b)
                pe.wait_ge(w_lo_ready[s], n + 1)
                for j in range(4):
                    u = U_OUT + 4 * b + j
                    proj.claim(u)
                    unit(u, s, BT, j // 2, mix_hi, mix_lo, j % 2, ready=mix_ready(j) if b == 0 and j < 2 else None)

            wd_h = w_hi[S_DOWN][:].rearrange("p (k n) -> p k n", n=D)
            wd_l = w_lo[S_DOWN][:].rearrange("p (k n) -> p k n", n=D)

            def ffn_group(i, first=False):
                pe.wait_ge(w_lo_ready[S_GATE], i + (FFN_USE[S_GATE] + 1))
                for n in range(4):
                    for half, s in enumerate((S_GATE, S_UP)):
                        if (n, half) == (0, 1):
                            pe.wait_ge(w_lo_ready[S_UP], i + (FFN_USE[S_UP] + 1))
                        ready = None
                        if first and half == 0 and n < 2:
                            ready = lambda k: pe.wait_ge(f_lo_done, NC * k + n + 1)
                        pe.wait_ge(proj.drained, i * 8 + (U_FFN + 2 * n + half - 3))
                        unit(U_FFN + 2 * n + half, s, BT, n // 2, f_hi, f_lo, n % 2, ready=ready)
                        if first and (n, half) == (0, 0):
                            for c in range(NC):
                                token_sums(F_NORM2, c, (f_sum, 15 + c))
                                spread_rms(F_NORM2, 1, c)
                pe.wait_ge(w_lo_ready[S_DOWN], i + 1)
                for n in range(16):
                    m, c = n % KT, n // KT
                    if m == 0:
                        pe.wait_ge(gu_lo_ready, i * 4 + (3 + c))
                    pe.wait_ge(aux.drained, i * 16 + (F_DOWN + n - 3))
                    bank, cols = aux.bank(F_DOWN + n)[:], slice(m * P, (m + 1) * P)
                    for k in range(BT):
                        last_mm = split3(bank, wd_h[:, k, cols], wd_l[:, k, cols], gu_hi[:, k, both(c)],
                                         gu_lo[:, k, both(c)], k == 0, k == BT - 1)
                    last_mm.then_inc(aux.filled, 1)

            ffn_group(0, first=True)
            with pe.Fori(1, GROUPS) as i:
                ffn_group(i)

            for b in range(4):
                s, use = ple_slot(b)
                pe.wait_ge(w_lo_ready[s], use + 1)
                for j in range(4):
                    n = 4 * b + j
                    proj.claim(U_PLE + 2 * n)
                    unit(U_PLE + 2 * n, s, BT, j // 2, e_hi, e_lo, j % 2,
                         ready=(lambda k: pe.wait_ge(e_lo_done, KT * j + k + 1)) if n < 2 else None)
                    if n == 0:
                        pe.wait_ge(p_lo_done, PLE // P)
                        token_sums(F_NORM3, 0, (e_sum, 8))
                        spread_rms(F_NORM3, 2, 0)
                    if j == 0:
                        pe.wait_ge(w_lo_ready[2], GROUPS + b + 1)
                    proj.claim(U_PLE + 2 * n + 1)
                    unit(U_PLE + 2 * n + 1, 2, BT, j // 2, p_hi, p_lo, j % 2, kts=PLE // P)
                    if n == 0:
                        token_sums(F_NORM3, 1, (e_sum, 16))
                        spread_rms(F_NORM3, 2, 1)
            for c in range(NC):
                token_sums(F_NORM4, c, (y_sum, 15 + c))
                spread_rms(F_NORM4, 3, c)


_INS = ['x_t', 'p_t', 'gains_in', 'w_in', 'w_gate_lr', 'b_gate', 'w_pool', 'w_out', 'w_ffn_gate', 'w_ffn_up', 'w_ffn_down',
        'w_ple_gate', 'w_ple_proj', 'consts']
_OUTS = [((KT, P, T), 'float32')]


def laid_out(inputs):
    import numpy as np

    a = {n: np.asarray(v) for n, v in inputs.items()}

    def block(w, c0, n):
        return w[:, c0:c0 + n].reshape(-1, P, n).transpose(1, 0, 2).reshape(P, -1)

    def column_blocks(w):
        return np.stack([block(w, c, BW) for c in range(0, w.shape[1], BW)])

    return {
        'x_t': np.ascontiguousarray(a['x'][0].T).reshape(KT, P, T),
        'p_t': np.ascontiguousarray(a['p'][0, 0].T).reshape(PLE // P, P, T),
        'gains_in': np.concatenate([a[n].reshape(-1, P).T for n in
                                    ('ln_mix', 'ln_ffn', 'ln_ple', 'ln_final', 'pool_scale', 'gla_norm')], axis=1),
        'w_in': np.concatenate([block(a['w_in'][0], c0, tiles * P) for c0, tiles in BLOCKS_IN], axis=1),
        'w_gate_lr': a['w_gate_lr'], 'b_gate': a['b_gate'], 'w_pool': a['w_pool'],
        'w_out': column_blocks(a['w_out'][0]),
        'w_ffn_gate': column_blocks(a['w_ffn_gate'][0]),
        'w_ffn_up': column_blocks(a['w_ffn_up'][0]),
        'w_ffn_down': a['w_ffn_down'][0].reshape(GROUPS, BT, P, D).transpose(0, 2, 1, 3).reshape(GROUPS, P, BT * D),
        'w_ple_gate': column_blocks(a['w_ple_gate'][0]),
        'w_ple_proj': column_blocks(a['w_ple_proj'][0]),
        'consts': const_rows(),
    }


def kernel(**inputs):
    import numpy as _np
    import concourse.bacc as _bacc
    from concourse import mybir as _mybir
    from concourse.bass_utils import run_bass_kernel_spmd as _run

    nc = _bacc.Bacc("TRN2", target_bir_lowering=False, num_devices=1, dynamic_dma_scratch_size=1024)
    arrays, args = {}, []
    given = laid_out(inputs)
    for name in _INS:
        a = _np.ascontiguousarray(given[name])
        arrays[f"in_{name}_dram"] = a
        args.append(nc.dram_tensor(f"in_{name}_dram", a.shape, _mybir.dt.from_np(a.dtype), kind="ExternalInput").ap())
    for i, (shape, dtype) in enumerate(_OUTS):
        dt = _mybir.dt.from_np(_np.dtype(dtype))
        args.append(nc.dram_tensor(f"out_{i}_dram", shape, dt, kind="ExternalOutput").ap())
    hybrid_block(nc, *args)
    r = _run(nc, [arrays], core_ids=[0])
    got = tuple(r.results[0][f"out_{i}_dram"] for i in range(len(_OUTS)))
    return _np.ascontiguousarray(got[0].reshape(D, T).T).reshape(1, T, D)
```

```python
from contextlib import ExitStack

import concourse.bass as bass
from concourse import mybir

F32 = mybir.dt.float32
F32R = mybir.dt.float32r
U32 = mybir.dt.uint32
ALU = mybir.AluOpType
ACT = mybir.ActivationFunctionType

P = 128
T = 1024
D = 1024
KT = D // P
TC = 512
NC = T // TC
C = 128
NCH = T // C
HEADS, DK, DV = 4, 64, 128
KEY, VAL = HEADS * DK, HEADS * DV
KP = KEY // P
RANK = 16
PLE = 256
FF = 2816
BW = 256
BT = BW // P
WINDOWS = (2, 4, 8, 16)
NG = len(WINDOWS)
EPS = 1e-6
LEVELS = (64, 32, 16, 8, 4, 2, 1)
NEAR = len(LEVELS) - 1
GROUPS = FF // BW
KB = 1024

OFF_V, OFF_G, OFF_LR = 2 * KEY, 2 * KEY + VAL, 2 * KEY + 2 * VAL
OFF_U = OFF_LR + RANK
Z_Q, Z_K, Z_U, Z_G = 0, 2, 8, 12
BLOCKS_IN = [(OFF_LR, 1), (KEY, 2), (0, 2), (OFF_U, 2), (OFF_U + BW, 2), (OFF_V, 2), (OFF_V + BW, 2), (OFF_G, 2),
             (OFF_G + BW, 2)]
NB = len(BLOCKS_IN)
BLOCK_AT = [sum(KT * P * tiles for _, tiles in BLOCKS_IN[:b]) for b in range(NB + 1)]
Z_OF = {2: Z_Q, 3: Z_U, 4: Z_U + 2, 7: Z_G, 8: Z_G + 2}

FILLS_AFTER = {(1, 3): [("gate", n) for n in range(4)], (2, 3): [("dec", n) for n in range(4)]}
FILLS_AFTER[3, 1] = [("diag", 0)]
for _lev in range(NEAR):
    for _half in range(2):
        _at = (3 + (_lev + 1) // 2, 2 * ((_lev + 1) % 2) + _half)
        FILLS_AFTER[_at] = FILLS_AFTER.get(_at, []) + [(_lev, 2 * _half), (_lev, 2 * _half + 1)]
FILLS_AFTER[6, 2] = [("near", 0)]
for _j in range(4):
    FILLS_AFTER[7, _j] = ([("kt", 2 * _j), ("kt", 2 * _j + 1)] if _j < 2 else [("kv", 2 * _j - 4), ("kv", 2 * _j - 3)]
                          ) + [("y", 2 * _j), ("y", 2 * _j + 1)]
FILLS_AFTER[8, 0] = [("o", n) for n in range(4)]
FILLS_AFTER[8, 1] = [("o", n) for n in range(4, 8)]
FILLS_AFTER[8, 2] = [("ot", n) for n in range(4)]
FILLS_AFTER[NB, 0] = [("ot", n) for n in range(4, 8)]
NORM_FILLS = 2 * NC
FILL = {}
for _key in sorted(FILLS_AFTER):
    for _fill in FILLS_AFTER[_key]:
        FILL[_fill] = NORM_FILLS + len(FILL)
F_MIX_END = NORM_FILLS + len(FILL)


def const_rows():
    import numpy as np

    ident = np.eye(P, dtype=np.float32)
    tri = np.triu(np.ones((P, P), np.float32)) / 16.0
    masks = []
    for s in LEVELS:
        m = np.zeros((P, P // (2 * s), s), np.float32)
        for j in range(P):
            if j % (2 * s) < s:
                m[j, j // (2 * s), :] = 1.0
        masks.append(m.reshape(P, P // 2))
    inv = np.tile(1.0 / np.arange(1, 17, dtype=np.float32), (P, 1))
    return np.ascontiguousarray(np.concatenate([ident, tri] + masks + [inv], axis=1))


def hybrid_block(nc, x_t, p_t, gains_in, w_in, w_gate_lr, b_gate, w_pool, w_out, w_ffn_gate, w_ffn_up,
                 w_ffn_down, w_ple_gate, w_ple_proj, consts, out):
    ctx = ExitStack()
    with ctx:
        A0 = 2 * KB
        B0, H0, W0, S0 = A0 + 64 * KB, A0 + 128 * KB, A0 + 160 * KB, A0 + 208 * KB

        def at(name, shape, offset, dt=F32):
            return nc.alloc_sbuf_tensor_at(name, shape, dt, offset=offset)

        a_hi = at("a_hi", [P, KT, T], A0, F32R)
        a_lo = at("a_lo", [P, KT, T], A0 + 32 * KB, F32R)
        mix_hi = at("mix_hi", [P, KT, T], A0, F32R)
        mix_lo = at("mix_lo", [P, KT, T], A0 + 32 * KB, F32R)
        gu_hi = at("gu_hi", [P, BT, T], A0 + 24 * KB, F32R)
        gu_lo = at("gu_lo", [P, BT, T], A0 + 32 * KB, F32R)
        p_raw = at("p_raw", [P, PLE // P, T], A0 + 40 * KB)
        gate_t = at("gate_t", [P, 2, TC], A0 + 48 * KB)
        up_t = at("up_t", [P, 2, TC], A0 + 52 * KB)
        ple_t = at("ple_t", [P, 2, TC], A0 + 40 * KB)
        p_hi = at("p_hi", [P, PLE // P, T], A0 + 48 * KB, F32R)
        p_lo = at("p_lo", [P, PLE // P, T], A0 + 56 * KB, F32R)
        z = at("z", [P, 16, T], B0)
        pre = at("pre", [P, NCH, KEY], B0 + 48 * KB)
        soft = at("soft", [P, NCH, KEY], B0 + 56 * KB)
        decay = at("decay", [P, KP, T], B0 + 56 * KB)
        lr = at("lr", [RANK + 1, T], B0 + 16 * KB)
        tri = at("tri", [P, P], B0 + 20 * KB)
        w_gl = at("w_gl", [RANK + 1, KEY], B0 + 21 * KB)
        v_tok = at("v_tok", [P, NCH, VAL], B0 + 16 * KB)
        window = at("window", [P, 2, T], B0 + 48 * KB)
        gated = at("gated", [P, HEADS, T], B0)
        f_hi = at("f_hi", [P, KT, T], B0, F32R)
        f_lo = at("f_lo", [P, KT, T], B0 + 32 * KB, F32R)
        e_hi = at("e_hi", [P, KT, T], B0, F32R)
        e_lo = at("e_lo", [P, KT, T], B0 + 32 * KB, F32R)
        h = at("h", [P, KT, T], H0)
        scaled = at("scaled", [P, 2, KP * T], H0)
        attn = at("attn", [P, 2, NCH, KP, C], H0 + 16 * KB)
        state = at("state", [P, NCH, KP, DV], H0)
        k_tok = at("k_tok", [P, NCH, KEY], H0 + 8 * KB)
        o_tok = at("o_tok", [P, 2, NCH, KP, DV], H0 + 16 * KB)
        slot_at = [W0, W0 + 24 * KB, A0]
        w_raw = [at(f"w_raw{s}", [P, KT * BW], o) for s, o in enumerate(slot_at)]
        w_hi = [at(f"w_hi{s}", [P, KT * BW], o + 8 * KB, F32R) for s, o in enumerate(slot_at)]
        w_lo = [at(f"w_lo{s}", [P, KT * BW], o + 16 * KB, F32R) for s, o in enumerate(slot_at)]
        small = [S0]

        def sm(name, shape, dt=F32):
            t = at(name, shape, small[0], dt)
            n = 4
            for d in shape[1:]:
                n *= d
            small[0] += (n + 31) // 32 * 32
            return t

        rms_all = sm("rms_all", [P, T])
        sums = sm("sums", [P, T])
        ident = sm("ident", [P, P])
        ones = sm("ones", [P, P])
        gains_all = sm("gains_all", [P, 4 * KT + NG + 1])
        gains = gains_all[:, 0:4 * KT].rearrange("p (n k) -> p n k", k=KT)
        g_pool, g_gla = gains_all[:, 4 * KT:4 * KT + NG], gains_all[:, 4 * KT + NG:4 * KT + NG + 1]
        stat = sm("stat", [P, 4, KT])
        head_ones = sm("head_ones", [P, 2])
        o_sq = at("o_sq", [P, 2, TC], S0 + 4 * KB)
        squares = at("squares", [P, 2, TC], small[0])
        w_pl = sm("w_pl", [P, NG, P])
        masks = sm("masks", [P, len(LEVELS), P // 2])
        inv_t = sm("inv_t", [P, 16])
        head_t = sm("head_t", [P, 16])
        last = sm("last", [P, KP, NCH])
        o_stat = sm("o_stat", [P, 3, NCH * HEADS])
        assert small[0] <= nc.sbuf_usable_end, small[0]

        pb = [ctx.enter_context(nc.psum_tensor(f"pb{i}", [P, TC], F32)) for i in range(8)]

        def sem(name):
            return ctx.enter_context(nc.semaphore(name))

        class Ring:

            def __init__(self, name, first):
                self.filled, self.drained, self.first = sem(name + "_filled"), sem(name + "_drained"), first

            def bank(self, n):
                return pb[self.first + n % 4]

            def claim(self, n):
                if not isinstance(n, int) or n >= 4:
                    nc.tensor.wait_ge(self.drained, n - 3)

        def u_in(b):
            return 6 + 4 * (b - 2)

        U_OUT = u_in(NB)
        U_FFN = U_OUT + 16
        U_PLE = U_FFN + 8 * GROUPS
        F_NORM1, F_NORM2 = 0, F_MIX_END
        F_DOWN = F_NORM2 + NORM_FILLS
        F_NORM3 = F_DOWN + 16 * GROUPS
        F_NORM4 = F_NORM3 + NORM_FILLS
        proj, aux = Ring("proj", 0), Ring("aux", 4)

        w_landed = [sem(f"w_landed{s}") for s in range(3)]
        w_hi_ready = [sem(f"w_hi_ready{s}") for s in range(3)]
        w_lo_ready = [sem(f"w_lo_ready{s}") for s in range(3)]
        x_landed = [sem(f"x_landed{n}") for n in range(16)]
        small_landed, ident_landed, gate_w_landed, mixer_landed, p_landed = (
            sem("small_landed"), sem("ident_landed"), sem("gate_w_landed"), sem("mixer_landed"), sem("p_landed"))
        x_back, out_stored = [sem(f"x_back{k}") for k in range(KT)], sem("out_stored")
        ones_ready, lr_ones = sem("ones_ready"), sem("lr_ones")
        first_hi, first_lo = sem("first_hi"), sem("first_lo")
        x_hi_done, x_lo_done, x_sq, x_sum = sem("x_hi_done"), sem("x_lo_done"), sem("x_sq"), sem("x_sum")
        root_ready, recip_ready, diag_ready = sem("root_ready"), sem("recip_ready"), sem("diag_ready")
        soft_ready, log_ready, last_ready = sem("soft_ready"), sem("log_ready"), sem("last_ready")
        diff_ready, exp_ready, scaled_ready, exp_b_ready, q_ready = (
            sem("diff_ready"), sem("exp_ready"), sem("scaled_ready"), sem("exp_b_ready"), sem("q_ready"))
        qk_ready, diag_part, near_ready, near_part = (
            sem("qk_ready"), sem("diag_part"), sem("near_ready"), sem("near_part"))
        kv_step, silu_ready = sem("kv_step"), sem("silu_ready")
        window_step, window_ready, pooled_ready = sem("window_step"), sem("window_ready"), sem("pooled_ready")
        y_hi, y_lo = sem("y_hi"), sem("y_lo")
        o_squared, o_var, o_root, o_recip, o_scaled, o_hi, o_lo = (
            sem("o_squared"), sem("o_var"), sem("o_root"), sem("o_recip"), sem("o_scaled"), sem("o_hi"), sem("o_lo"))
        f_hi_done, f_lo_done, f_sq, f_sum = sem("f_hi_done"), sem("f_lo_done"), sem("f_sq"), sem("f_sum")
        gate_silu, gu_ready, gu_hi_ready, gu_lo_ready = (
            sem("gate_silu"), sem("gu_ready"), sem("gu_hi_ready"), sem("gu_lo_ready"))
        e_hi_done, e_lo_done, e_sq, e_sum = sem("e_hi_done"), sem("e_lo_done"), sem("e_sq"), sem("e_sum")
        p_hi_done, p_lo_done, ple_sig, h_final, y_sq, y_sum, h_gained, y_first, y_second = (
            sem("p_hi_done"), sem("p_lo_done"), sem("ple_sig"), sem("h_final"), sem("y_sq"), sem("y_sum"), sem("h_gained"),
            sem("y_first"), sem("y_second"))

        block = ctx.enter_context(nc.Block())

        def in_tile(b, j):
            return (j % 2, j // 2) if b == NB - 1 else (j // 2, j % 2)

        def out_tile(n):
            return (n % 2, n // 2) if n < 4 else (n // NC, n % NC)

        OUT_AT = {out_tile(n): n for n in range(16)}

        def pair_order(n, half):
            return 4 * (n // 2) + 2 * half + n % 2

        def ple_tile(n):
            return (n // NC, n % NC) if n < 12 else (6 + n % 2, (n - 12) // 2)

        def both(c):
            return slice(c * TC, (c + 1) * TC)

        def slot_of(b):
            return b % 2, b // 2

        S_GATE, S_UP, S_DOWN = 1, 0, 2
        FFN_USE = {S_UP: 7, S_GATE: 6, S_DOWN: 0}
        assert (NB + 4) // 2 == 6 and (NB + 5) // 2 == 7

        def ple_slot(b):
            s = (S_GATE, S_UP)[b % 2]
            return s, FFN_USE[s] + GROUPS + b // 2

        @block.sync
        def _(sp):
            def load(s, n, dst, src):
                if not (isinstance(n, int) and n == 0):
                    sp.wait_ge(w_lo_ready[s], n)
                sp.dma_start(dst, src).then_inc(w_landed[s], 16)

            def block_load(b):
                s, n = slot_of(b)
                if b < NB:
                    size = KT * P * BLOCKS_IN[b][1]
                    load(s, n, w_raw[s][:, 0:size], w_in[:, BLOCK_AT[b]:BLOCK_AT[b] + size])
                else:
                    load(s, n, w_raw[s][:], w_out[b - NB])

            sp.dma_start(gains_all[:], gains_in).then_inc(small_landed, 16)
            for n in range(16):
                k, c = n % KT, n // KT
                sp.dma_start(h[:, k, both(c)], x_t[k][:, both(c)]).then_inc(x_landed[n], 16)
                if n == 1:
                    block_load(0)
                if n == 7:
                    block_load(1)
                    sp.dma_start(ident[:], consts[:, 0:P]).then_inc(ident_landed, 16)
            block_load(2)
            sp.dma_start(tri[:], consts[:, P:2 * P]).then_inc(gate_w_landed, 16)
            sp.dma_start(w_gl[0:RANK, :], w_gate_lr[0]).then_inc(gate_w_landed, 16)
            sp.dma_start(w_gl[RANK:RANK + 1, :], b_gate).then_inc(gate_w_landed, 16)
            sp.wait_ge(x_sum, 16)
            nm = len(LEVELS) * P // 2
            sp.dma_start(masks[:], consts[:, 2 * P:2 * P + nm].rearrange("p (l n) -> p l n", n=P // 2)
                         ).then_inc(mixer_landed, 16)
            sp.dma_start(inv_t[:], consts[:, 2 * P + nm:]).then_inc(mixer_landed, 16)
            sp.dma_start(w_pl[:], w_pool[0].rearrange("g c d -> c g d")).then_inc(mixer_landed, 16)
            for b in range(3, NB + 2):
                block_load(b)

            def residual(k):
                sp.dma_start(h[:, k, :], x_t[k]).then_inc(x_back[k], 16)

            sp.wait_ge(aux.filled, FILL["o", 7] + 1)
            for k in range(KT // 2):
                residual(k)
            sp.wait_ge(o_scaled, 8)
            sp.wait_ge(aux.filled, F_MIX_END)
            for k in range(KT // 2, KT):
                residual(k)
            for b in range(NB + 2, NB + 4):
                block_load(b)

            def ffn_in(i):
                load(S_GATE, FFN_USE[S_GATE] + i, w_raw[S_GATE][:], w_ffn_gate[bass.ds(i, 1)].rearrange("g p n -> p (g n)"))
                load(S_UP, FFN_USE[S_UP] + i, w_raw[S_UP][:], w_ffn_up[bass.ds(i, 1)].rearrange("g p n -> p (g n)"))

            def ffn_down(i):
                load(S_DOWN, i, w_raw[S_DOWN][:], w_ffn_down[bass.ds(i, 1)].rearrange("g p n -> p (g n)"))

            ffn_in(0)
            sp.wait_ge(proj.filled, U_FFN)
            sp.dma_start(p_raw[:], p_t.rearrange("k p t -> p k t")).then_inc(p_landed, 16)
            ffn_down(0)
            with sp.Fori(0, GROUPS - 1) as i:
                ffn_in(i + 1)
                ffn_down(i + 1)
            for b in range(4):
                s, n = ple_slot(b)
                load(s, n, w_raw[s][:], w_ple_gate[b])
                load(2, GROUPS + b, w_raw[2][:, 0:2 * BW], w_ple_proj[b])
            for c, normed in enumerate((y_first, y_second)):
                for k in range(KT):
                    sp.wait_ge(normed, k + 1)
                    sp.dma_start(out[k][:, both(c)], h[:, k, both(c)]).then_inc(out_stored, 16)
            sp.wait_ge(out_stored, 16 * NC * KT)

        @block.gpsimd
        def _(pool):
            def lo_half(s, n, size):
                pool.wait_ge(w_hi_ready[s], n + 1)
                nc.gpsimd.tensor_tensor(w_lo[s][:, 0:size], w_raw[s][:, 0:size], w_hi[s][:, 0:size].bitcast(F32),
                                        ALU.subtract).then_inc(w_lo_ready[s], 1)

            nc.gpsimd.memset(ones[:], 1.0).then_inc(ones_ready, 1)
            for r in range(2):
                for col in range(2):
                    pool.wait_ge(ones_ready, 1 + 2 * r + col)
                    nc.gpsimd.memset(head_ones[r * DK:(r + 1) * DK, col:col + 1], float(r == col)).then_inc(ones_ready, 1)
            pool.wait_ge(ones_ready, 5)
            nc.gpsimd.memset(lr[:], 1.0).then_inc(lr_ones, 1)
            steps = [0]

            def joined():
                pool.wait_ge(window_step, steps[0])

            def windowed(g):
                pool.wait_ge(proj.drained, u_in(3) + 2 * (g + 1))
                if g:
                    pool.wait_ge(pooled_ready, 2 * g)
                src = z[:, Z_U + g, :]
                for d in range(g + 1):
                    sh, dst = 1 << d, window[:, d % 2, :]
                    if d:
                        joined()
                    nc.gpsimd.tensor_tensor(dst[:, sh:T], src[:, sh:T], src[:, 0:T - sh], ALU.add).then_inc(window_step, 1)
                    nc.gpsimd.tensor_copy(dst[:, 0:sh], src[:, 0:sh]).then_inc(window_step, 1)
                    steps[0] += 2
                    src = dst
                joined()
                w = WINDOWS[g]
                nc.gpsimd.tensor_tensor(head_t[:, 0:w], src[:, 0:w], inv_t[:, 0:w], ALU.mult).then_inc(window_ready, 1)

            def block_lo(b):
                s, n = slot_of(b)
                lo_half(s, n, KT * (P * BLOCKS_IN[b][1] if b < NB else BW))

            block_lo(0)
            half = KT * BW // 2
            pool.wait_ge(w_hi_ready[1], 1)
            nc.gpsimd.tensor_tensor(w_lo[1][:, half:], w_raw[1][:, half:], w_hi[1][:, half:].bitcast(F32), ALU.subtract
                                    ).then_inc(w_lo_ready[1], 1)
            for b in range(2, 6):
                block_lo(b)
            pool.wait_ge(mixer_landed, 16 * 3)
            windowed(0)
            windowed(1)
            block_lo(6)
            windowed(2)
            block_lo(7)
            windowed(3)
            block_lo(8)
            block_lo(NB)
            for c in range(NC):
                pool.wait_ge(y_hi, c + 1)
                nc.gpsimd.tensor_tensor(mix_lo[:, HEADS:KT, both(c)], z[:, Z_U:Z_U + NG, both(c)],
                                        mix_hi[:, HEADS:KT, both(c)].bitcast(F32), ALU.subtract).then_inc(y_lo, 1)
            for b in range(NB + 1, NB + 4):
                block_lo(b)
            with pool.Fori(0, GROUPS) as i:
                for s in (S_GATE, S_UP, S_DOWN):
                    lo_half(s, FFN_USE[s] + i, KT * BW)
            lo_half(*ple_slot(0), KT * BW)
            for n in range(16):
                total, sq = sums[:, both(n // KT)], squares[:, n % 2, :]
                pool.wait_ge(e_sq, n + 1)
                if n % KT == 0:
                    nc.gpsimd.tensor_copy(total, sq).then_inc(e_sum, 1)
                else:
                    pool.wait_ge(e_sum, n)
                    nc.gpsimd.tensor_tensor(total, total, sq, ALU.add).then_inc(e_sum, 1)
            for b in range(4):
                lo_half(2, GROUPS + b, 2 * BW)
                if b < 3:
                    lo_half(*ple_slot(b + 1), KT * BW)
            pool.wait_ge(aux.drained, F_NORM4 + 2)
            pool.wait_ge(h_gained, 14)
            for m in range(KT):
                nc.gpsimd.tensor_tensor(h[:, m, both(0)], h[:, m, both(0)], rms_all[:, both(0)], ALU.mult
                                        ).then_inc(y_first, 1)

        @block.scalar
        def _(act):
            def hi_weights(s, n, size, used=None):
                act.wait_ge(w_landed[s], n * 16 + 16)
                if used is not None:
                    act.wait_ge(*used)
                nc.scalar.copy(w_hi[s][:, 0:size], w_raw[s][:, 0:size]).then_inc(w_hi_ready[s], 1)

            def block_hi(b):
                s, n = slot_of(b)
                used = None
                if b >= 2:
                    used = (proj.filled, {2: 4, 3: 6}.get(b, u_in(b - 1) if b < NB + 2 else U_OUT + 4 * (b - NB - 1)))
                hi_weights(s, n, KT * (P * BLOCKS_IN[b][1] if b < NB else BW), used)

            def root(norm, c):
                act.wait_ge(aux.drained, (F_NORM1, F_NORM2, F_NORM3, F_NORM4)[norm] + 2 * c + 1)
                nc.scalar.activation(stat[:, 1, 4 * c:4 * c + 4], stat[:, 0, 4 * c:4 * c + 4], ACT.Sqrt
                                     ).then_inc(root_ready, 1)

            def hi_tile(m, c, gain, hi, hi_sem):
                nc.scalar.activation(hi[:, m, both(c)], h[:, m, both(c)], ACT.Copy,
                                     scale=gains[:, gain, m:m + 1]).then_inc(hi_sem, 1)

            def square(n, m, c, sq_sem, sum_sem):
                if n >= 2:
                    act.wait_ge(sum_sem, n - 1)
                nc.scalar.activation(squares[:, n % 2, :], h[:, m, both(c)], ACT.Square).then_inc(sq_sem, 1)

            act.wait_ge(small_landed, 16)
            for n in range(KT):
                if n == 2:
                    block_hi(0)
                act.wait_ge(x_landed[n], 16)
                hi_tile(n, 0, 0, a_hi, x_hi_done)
            half = KT * BW // 2
            act.wait_ge(w_landed[1], 16)
            nc.scalar.copy(w_hi[1][:, 0:half], w_raw[1][:, 0:half]).then_inc(first_hi, 1)
            nc.scalar.copy(w_hi[1][:, half:], w_raw[1][:, half:]).then_inc(w_hi_ready[1], 1)
            for n in range(KT):
                square(n, n, 0, x_sq, x_sum)
            for n in range(KT, 16):
                if n == 12:
                    root(0, 0)
                act.wait_ge(x_landed[n], 16)
                hi_tile(n - KT, 1, 0, a_hi, x_hi_done)
                square(n, n - KT, 1, x_sq, x_sum)
            root(0, 1)
            block_hi(2)
            act.wait_ge(aux.drained, FILL["gate", 3] + 1)
            nc.scalar.activation(soft[:], pre[:], ACT.Abs).then_inc(soft_ready, 1)
            act.wait_ge(soft_ready, 1)
            nc.scalar.activation(soft[:], soft[:], ACT.Exp, scale=-1.0).then_inc(soft_ready, 1)
            act.wait_ge(soft_ready, 2)
            nc.scalar.activation(soft[:], soft[:], ACT.Ln, bias=1.0).then_inc(soft_ready, 1)
            block_hi(3)

            def exp_diff(lev):
                act.wait_ge(diff_ready, 2 * (lev + 1) if lev < len(LEVELS) else 2 * len(LEVELS) + 1)
                nc.scalar.activation(scaled[:, lev % 2, :], scaled[:, lev % 2, :], ACT.Exp).then_inc(exp_ready, 1)

            exp_diff(0)
            act.wait_ge(aux.drained, FILL["dec", 3] + 1)
            nc.scalar.activation(last[:], decay[:].rearrange("p a (t c) -> p a t c", c=C)[:, :, :, C - 1], ACT.Exp
                                 ).then_inc(last_ready, 1)
            exp_diff(1)
            for b in range(4, 7):
                block_hi(b)
                exp_diff(2 * b - 6)
                exp_diff(2 * b - 5)
            block_hi(7)
            act.wait_ge(aux.filled, FILL["near", 0] + 1)
            nc.scalar.activation(scaled[:, 0, :], decay[:].rearrange("p a t -> p (a t)"), ACT.Exp).then_inc(exp_b_ready, 1)

            def silu_unit(b, j):
                act.wait_ge(proj.drained, u_in(b) + j + 1)
                m, c = in_tile(b, j)
                g = z[:, Z_OF[b] + m, both(c)]
                nc.scalar.activation(g, g, ACT.Silu).then_inc(silu_ready, 1)

            def square_o(f):
                act.wait_ge(aux.drained, FILL["o", f] + 1)
                if f >= 2:
                    act.wait_ge(o_squared, f - 1)
                for q in range(4):
                    i = nc.scalar.activation(o_sq[:, f % 2, q * DV:(q + 1) * DV],
                                             o_tok[:, f % 2, 2 * (f // 2) + q // 2, q % 2, :], ACT.Square,
                                             accum_out=o_stat[:, 0, 4 * f + q:4 * f + q + 1])
                i.then_inc(o_squared, 1)

            for j in range(4):
                silu_unit(7, j)
                if j == 0:
                    block_hi(8)
            def o_root_of(c):
                act.wait_ge(o_var, c + 1)
                nc.scalar.activation(o_stat[:, 2, 16 * c:16 * c + 16], o_stat[:, 1, 16 * c:16 * c + 16], ACT.Sqrt
                                     ).then_inc(o_root, 1)

            def mix_hi_y(c):
                act.wait_ge(aux.drained, FILL["y", 7] + 1)
                act.wait_ge(proj.filled, u_in(8) + 2 * c + 2)
                nc.scalar.copy(mix_hi[:, HEADS:KT, both(c)], z[:, Z_U:Z_U + NG, both(c)]).then_inc(y_hi, 1)

            def mix_hi_o(c):
                for hd in range(HEADS):
                    act.wait_ge(aux.drained, FILL["ot", 4 * c + hd] + 1)
                    nc.scalar.copy(mix_hi[:, hd, both(c)], gated[:, hd, both(c)]).then_inc(o_hi, 1)

            silu_unit(8, 0)
            for f in range(4):
                square_o(f)
            silu_unit(8, 1)
            o_root_of(0)
            block_hi(NB)
            mix_hi_y(0)
            for f in range(4, 8):
                square_o(f)
            o_root_of(1)
            silu_unit(8, 2)
            mix_hi_o(0)
            silu_unit(8, 3)
            mix_hi_y(1)
            block_hi(NB + 1)
            mix_hi_o(1)

            for n in range(16):
                if n in (4, 8):
                    block_hi(NB + 1 + n // 4)
                if n == 12:
                    hi_weights(S_GATE, FFN_USE[S_GATE], KT * BW, (proj.filled, U_OUT + 12))
                act.wait_ge(proj.drained, U_OUT + n + 1)
                hi_tile(*out_tile(n), 1, f_hi, f_hi_done)
                square(n, *out_tile(n), f_sq, f_sum)
            hi_weights(S_UP, FFN_USE[S_UP], KT * BW, (proj.filled, U_FFN))
            root(1, 0)
            root(1, 1)
            hi_weights(S_DOWN, 0, KT * BW)

            def ffn_silu(i, n):
                act.wait_ge(proj.drained, i * 8 + (U_FFN + pair_order(n, 0) + 1))
                nc.scalar.activation(gate_t[:, n % 2, :], gate_t[:, n % 2, :], ACT.Silu).then_inc(gate_silu, 1)

            def ffn_hi(i, n):
                act.wait_ge(gu_ready, i * 4 + (n + 1))
                nc.scalar.copy(gu_hi[:, n // 2, both(n % 2)], up_t[:, n % 2, :]).then_inc(gu_hi_ready, 1)

            def ffn_pair(i, pair):
                for step in (ffn_silu, ffn_hi):
                    for n in (2 * pair, 2 * pair + 1):
                        step(i, n)

            with act.Fori(0, GROUPS - 1) as i:
                ffn_pair(i, 0)
                ffn_pair(i, 1)
                hi_weights(S_GATE, i + (FFN_USE[S_GATE] + 1), KT * BW, (proj.filled, i * 8 + (U_FFN + pair_order(3, 0) + 1)))
                hi_weights(S_UP, i + (FFN_USE[S_UP] + 1), KT * BW, (proj.filled, i * 8 + (U_FFN + 8)))
                hi_weights(S_DOWN, i + 1, KT * BW, (aux.filled, i * 16 + (F_DOWN + 16)))
            last_group = GROUPS - 1
            ffn_pair(last_group, 0)
            ffn_silu(last_group, 2)
            ffn_silu(last_group, 3)
            hi_weights(*ple_slot(0), KT * BW, (proj.filled, U_PLE - 8 + pair_order(3, 0) + 1))
            ffn_hi(last_group, 2)
            ffn_hi(last_group, 3)
            for n in range(16):
                act.wait_ge(aux.drained, F_NORM3 - 16 + n + 1)
                hi_tile(n % KT, n // KT, 2, e_hi, e_hi_done)
                square(n, n % KT, n // KT, e_sq, e_sum)
            act.wait_ge(p_landed, 16)
            for k in range(PLE // P):
                nc.scalar.copy(p_hi[:, k, :], p_raw[:, k, :]).then_inc(p_hi_done, 1)
            hi_weights(2, GROUPS, 2 * BW, (aux.filled, F_NORM3))
            root(2, 0)
            hi_weights(*ple_slot(1), KT * BW, (proj.filled, U_PLE))
            root(2, 1)
            for pair in range(8):
                b, ns = pair // 2, (2 * pair, 2 * pair + 1)
                if pair % 2 == 0 and b > 0:
                    hi_weights(2, GROUPS + b, 2 * BW, (proj.filled, U_PLE + 8 * b))
                    if b < 3:
                        hi_weights(*ple_slot(b + 1), KT * BW, (proj.filled, U_PLE + 8 * b - 2))
                for n in ns:
                    act.wait_ge(proj.drained, U_PLE + pair_order(n, 0) + 1)
                    nc.scalar.activation(ple_t[:, n % 2, :], ple_t[:, n % 2, :], ACT.Sigmoid).then_inc(ple_sig, 1)
                    if n == 14:
                        root(3, 0)
                if pair == 7:
                    nc.scalar.activation(stat[:, 2, 0:1], stat[:, 0, 0:1], ACT.Sqrt)
                for n in ns:
                    m, c = ple_tile(n)
                    act.wait_ge(h_final, n + 1)
                    square(n, m, c, y_sq, y_sum)
                    act.wait_ge(y_sq, n + 1)
                    nc.scalar.activation(h[:, m, both(c)], h[:, m, both(c)], ACT.Copy, scale=gains[:, 3, m:m + 1]
                                         ).then_inc(h_gained, 1)
            root(3, 1)

        @block.vector
        def _(dve):
            V = nc.vector

            def norm_var(f0, c):
                dve.wait_ge(aux.filled, f0 + 2 * c + 1)
                V.tensor_scalar(stat[:, 0, 4 * c:4 * c + 4], aux.bank(f0 + 2 * c)[:, 0:4], 1.0 / D, EPS, ALU.mult, ALU.add
                                ).then_inc(aux.drained, 1)

            def norm_diag(norm, c):
                dve.wait_ge(root_ready, 2 * norm + c + 1)
                r = stat[:, 3, 4 * c:4 * c + 4]
                V.reciprocal(r, stat[:, 1, 4 * c:4 * c + 4]).then_inc(recip_ready, 1)
                dve.wait_ge(recip_ready, 2 * norm + c + 1)
                V.tensor_tensor(sums[:, both(c)].rearrange("p (t c) -> p t c", c=P),
                                ident[:].unsqueeze(1).broadcast_to([P, 4, P]),
                                r.unsqueeze(2).broadcast_to([P, 4, P]), ALU.mult).then_inc(diag_ready, 1)

            def norm_take(f0, c):
                f = f0 + 2 * c + 1
                dve.wait_ge(aux.filled, f + 1)
                V.tensor_copy(rms_all[:, both(c)], aux.bank(f)[:]).then_inc(aux.drained, 1)

            def norm_stats(f0, norm):
                for c in range(NC):
                    norm_var(f0, c)
                    norm_diag(norm, c)
                    norm_take(f0, c)
                dve.wait_ge(aux.drained, f0 + NORM_FILLS)

            def lo_tile(n, m, c, gain, hi, lo, hi_sem, lo_sem):
                dve.wait_ge(hi_sem, n + 1)
                V.scalar_tensor_tensor(out=lo[:, m, both(c)], in0=h[:, m, both(c)], scalar=gains[:, gain, m:m + 1],
                                       in1=hi[:, m, both(c)].bitcast(F32), op0=ALU.mult, op1=ALU.subtract
                                       ).then_inc(lo_sem, 1)

            def add_squares(n, m, c, sq_sem, sum_sem):
                dve.wait_ge(sq_sem, n + 1)
                if m == 0:
                    V.tensor_copy(sums[:, both(c)], squares[:, n % 2, :]).then_inc(sum_sem, 1)
                else:
                    dve.wait_ge(sum_sem, n)
                    V.tensor_tensor(sums[:, both(c)], sums[:, both(c)], squares[:, n % 2, :], ALU.add
                                    ).then_inc(sum_sem, 1)

            dve.wait_ge(small_landed, 16)
            for n in range(KT):
                dve.wait_ge(x_landed[n], 16)
                lo_tile(n, n, 0, 0, a_hi, a_lo, x_hi_done, x_lo_done)
            half = KT * BW // 2
            dve.wait_ge(first_hi, 1)
            V.tensor_tensor(w_lo[1][:, 0:half], w_raw[1][:, 0:half], w_hi[1][:, 0:half].bitcast(F32), ALU.subtract
                            ).then_inc(first_lo, 1)
            for n in range(KT):
                add_squares(n, n, 0, x_sq, x_sum)
            for n in range(KT, 16):
                if n == 10:
                    norm_var(F_NORM1, 0)
                if n == 13:
                    dve.wait_ge(ident_landed, 16)
                    norm_diag(0, 0)
                dve.wait_ge(x_landed[n], 16)
                lo_tile(n, n - KT, 1, 0, a_hi, a_lo, x_hi_done, x_lo_done)
                add_squares(n, n - KT, 1, x_sq, x_sum)
            norm_take(F_NORM1, 0)
            dve.wait_ge(aux.drained, F_NORM1 + 2)
            dve.wait_ge(lr_ones, 1)

            def lr_unit(u, c):
                dve.wait_ge(proj.filled, u + 1)
                V.tensor_tensor(lr[0:RANK, both(c)], proj.bank(u)[0:RANK, :], rms_all[0:RANK, both(c)], ALU.mult
                                ).then_inc(proj.drained, 1)

            def tile_unit(u, n, c):
                dve.wait_ge(proj.filled, u + 1)
                V.tensor_tensor(z[:, n, both(c)], proj.bank(u)[:], rms_all[:, both(c)], ALU.mult
                                ).then_inc(proj.drained, 1)

            def v_unit(b, j):
                u = u_in(b) + j
                dve.wait_ge(proj.filled, u + 1)
                V.tensor_tensor(v_tok[:, 2 * j:2 * j + 2, (b - 5) * BW:(b - 4) * BW],
                                proj.bank(u)[:].rearrange("p (t n) -> p t n", t=2),
                                stat[:, 3, 2 * j:2 * j + 2].unsqueeze(2).broadcast_to([P, 2, BW]), ALU.mult
                                ).then_inc(proj.drained, 1)

            lr_unit(0, 0)
            tile_unit(1, Z_K, 0)
            tile_unit(2, Z_K + 1, 0)
            norm_var(F_NORM1, 1)
            norm_diag(0, 1)
            norm_take(F_NORM1, 1)
            dve.wait_ge(aux.drained, F_NORM1 + 4)
            lr_unit(3, 1)
            tile_unit(4, Z_K, 1)
            tile_unit(5, Z_K + 1, 1)

            flat_b = decay[:].rearrange("p a t -> p (a t)")
            flat_k = z[:, Z_K:Z_K + KP, :].rearrange("p a t -> p (a t)")
            flat_q = z[:, Z_Q:Z_Q + KP, :].rearrange("p a t -> p (a t)")

            def halves(ap, s):
                v = ap.rearrange("p (n s) -> p n s", s=2 * s)
                return v[:, :, 0:s], v[:, :, s:2 * s]

            def level_diff(lev):
                s = LEVELS[lev]
                left, right = halves(flat_b, s)
                ref = flat_b.rearrange("p (n s) -> p n s", s=2 * s)[:, :, s - 1:s].broadcast_to([P, KP * T // (2 * s), s])
                o_left, o_right = halves(scaled[:, lev % 2, :], s)
                V.tensor_tensor(o_left, ref, left, ALU.subtract).then_inc(diff_ready, 1)
                V.tensor_tensor(o_right, right, ref, ALU.subtract).then_inc(diff_ready, 1)

            def level_scale(lev):
                s = LEVELS[lev]
                dve.wait_ge(exp_ready, lev + 1)
                o_left, o_right = halves(scaled[:, lev % 2, :], s)
                V.tensor_tensor(o_left, o_left, halves(flat_k, s)[0], ALU.mult).then_inc(scaled_ready, 1)
                V.scalar_tensor_tensor(out=o_right, in0=halves(flat_q, s)[1], scalar=DK ** -0.5, in1=o_right,
                                       op0=ALU.mult, op1=ALU.mult).then_inc(scaled_ready, 1)

            def qk_product():
                V.scalar_tensor_tensor(out=scaled[:, 1, :], in0=flat_q, scalar=DK ** -0.5, in1=flat_k, op0=ALU.mult,
                                       op1=ALU.mult).then_inc(qk_ready, 1)

            def near_product():
                dve.wait_ge(scaled_ready, 2 * (NEAR + 1))
                left, right = halves(scaled[:, NEAR % 2, :], LEVELS[NEAR])
                V.tensor_tensor(left, left, right, ALU.mult).then_inc(near_ready, 1)

            def k_diff():
                b4 = decay[:].rearrange("p a (t c) -> p (a t) c", c=C)
                V.tensor_tensor(scaled[:, 1, :].rearrange("p (n c) -> p n c", c=C),
                                b4[:, :, C - 1:C].broadcast_to([P, KP * NCH, C]), b4, ALU.subtract
                                ).then_inc(diff_ready, 1)

            def k_scale():
                dve.wait_ge(exp_ready, len(LEVELS) + 1)
                V.tensor_tensor(flat_k, flat_k, scaled[:, 1, :], ALU.mult).then_inc(scaled_ready, 1)

            kv_steps = [0]

            def drain(kind, n):
                f = FILL[kind, n]
                dve.wait_ge(aux.filled, f + 1)
                bank = aux.bank(f)[:]
                if kind == "gate":
                    i = V.tensor_copy(pre[:, 2 * n:2 * n + 2, :], bank.rearrange("p (t n) -> p t n", t=2))
                elif kind == "dec":
                    if n == 0:
                        dve.wait_ge(aux.filled, f + 4)
                    i = V.tensor_copy(decay[:, n // 2, both(n % 2)], bank)
                elif kind == "diag":
                    for r in range(2):
                        i = V.tensor_tensor(
                            attn[:, r].rearrange("p t a c -> p (t a) c"),
                            ident[:].unsqueeze(1).broadcast_to([P, NCH * KP, C]),
                            bank[:, 0:2 * NCH * KP].rearrange("p (n r) -> p n r", r=2)[:, :, r:r + 1].broadcast_to(
                                [P, NCH * KP, C]), ALU.mult)
                        if r == 0:
                            i.then_inc(diag_part, 1)
                elif kind == "near":
                    dve.wait_ge(aux.drained, f)
                    for r in range(2):
                        i = V.copy_predicated(
                            attn[:, r].rearrange("p t a (n s) -> p (t a) n s", s=2)[:, :, :, 1:2],
                            masks[:, NEAR, :].rearrange("p (n s) -> p n s", s=1).unsqueeze(1).broadcast_to(
                                [P, NCH * KP, C // 2, 1]).bitcast(U32),
                            bank[:, 0:2 * NCH * KP].rearrange("p (n r s) -> p n r s", r=2, s=1)[:, :, r:r + 1, :].broadcast_to(
                                [P, NCH * KP, C // 2, 1]))
                        if r == 0:
                            i.then_inc(near_part, 1)
                elif kind == "kt":
                    i = V.tensor_copy(k_tok[:, 2 * n:2 * n + 2, :], bank.rearrange("p (t c) -> p t c", t=2))
                elif kind == "y":
                    g, c = n // NC, n % NC
                    i = V.tensor_scalar(z[:, Z_U + g, both(c)], bank, g_pool[:, g:g + 1], None, ALU.mult)
                elif kind == "kv":
                    for t in range(2 * n, min(2 * n + 2, NCH - 1)):
                        part = bank[:, (t % 2) * 2 * DV:(t % 2 + 1) * 2 * DV].rearrange("p (a v) -> p a v", a=KP)
                        closing = t == min(2 * n + 1, NCH - 2)
                        if t == 0:
                            V.tensor_copy(state[:, 1, :, :], part).then_inc(kv_step, 1)
                            kv_steps[0] += 1
                            continue
                        dve.wait_ge(kv_step, kv_steps[0])
                        if t == 2 * n:
                            dve.wait_ge(aux.drained, f)
                        for a in range(KP):
                            i = V.scalar_tensor_tensor(
                                out=state[:, t + 1, a, :], in0=state[:, t, a, :], scalar=last[:, a, t:t + 1],
                                in1=part[:, a, :], op0=ALU.mult, op1=ALU.add)
                            if not (closing and a == KP - 1):
                                i.then_inc(kv_step, 1)
                                kv_steps[0] += 1
                elif kind == "o":
                    i = V.tensor_copy(o_tok[:, n % 2, 2 * (n // 2):2 * (n // 2) + 2, :, :].rearrange("p t a c -> p (t a) c"),
                                      bank.rearrange("p (q c) -> p q c", c=DV))
                elif kind == "ot":
                    c, hd = n // HEADS, n % HEADS
                    i = V.scalar_tensor_tensor(out=gated[:, hd, both(c)], in0=bank, scalar=g_gla,
                                               in1=z[:, Z_G + hd, both(c)], op0=ALU.mult, op1=ALU.mult)
                else:
                    s, r, c = LEVELS[kind], n % 2, n // 2
                    dst = attn[:, r, 4 * c:4 * c + 4, :, :].rearrange("p t a (n s) -> p (t a) n s", s=2 * s)
                    dst = dst[:, :, :, s:2 * s]
                    m = masks[:, kind, :].rearrange("p (n s) -> p n s", s=s).unsqueeze(1).broadcast_to(
                        [P, 4 * KP, C // (2 * s), s])
                    before = FILL["diag", 0] if kind == 0 else FILL[kind - 1, n]
                    if kind == 0:
                        dve.wait_ge(diag_part, 1)
                    dve.wait_ge(aux.drained, before + 1)
                    i = V.copy_predicated(dst, m.bitcast(U32), bank.rearrange("p (a n s) -> p a n s", a=4 * KP, s=s))
                i.then_inc(aux.drained, 1)

            def drains_after(b, j):
                for kind, n in FILLS_AFTER.get((b, j), []):
                    drain(kind, n)

            def pooled(g):
                w = WINDOWS[g]
                dve.wait_ge(window_ready, g + 1)
                V.scalar_tensor_tensor(out=z[:, Z_U + g, w:T], in0=window[:, g % 2, w:T], scalar=1.0 / w,
                                       in1=z[:, Z_U + g, w:T], op0=ALU.mult, op1=ALU.subtract).then_inc(pooled_ready, 1)
                V.tensor_tensor(z[:, Z_U + g, 0:w], head_t[:, 0:w], z[:, Z_U + g, 0:w], ALU.subtract
                                ).then_inc(pooled_ready, 1)

            def o_var_of(c):
                dve.wait_ge(o_squared, 4 * c + 4)
                V.tensor_scalar(o_stat[:, 1, 16 * c:16 * c + 16], o_stat[:, 0, 16 * c:16 * c + 16], 1.0 / DV, EPS,
                                ALU.mult, ALU.add).then_inc(o_var, 1)

            def o_scale(c):
                dve.wait_ge(o_root, c + 1)
                V.reciprocal(o_stat[:, 1, 16 * c:16 * c + 16], o_stat[:, 2, 16 * c:16 * c + 16]).then_inc(o_recip, 1)
                dve.wait_ge(o_recip, c + 1)
                for f in range(4 * c, 4 * c + 4):
                    ov = o_tok[:, f % 2, 2 * (f // 2):2 * (f // 2) + 2, :, :].rearrange("p t a c -> p (t a) c")
                    V.tensor_tensor(ov, ov, o_stat[:, 1, 4 * f:4 * f + 4].unsqueeze(2).broadcast_to([P, 4, DV]),
                                    ALU.mult).then_inc(o_scaled, 1)

            def o_low(n):
                c, hd = n // HEADS, n % HEADS
                dve.wait_ge(o_hi, n + 1)
                V.tensor_tensor(mix_lo[:, hd, both(c)], gated[:, hd, both(c)], mix_hi[:, hd, both(c)].bitcast(F32),
                                ALU.subtract).then_inc(o_lo, 1)

            dve.wait_ge(mixer_landed, 16 * 3)
            drains_after(1, 3)
            for j in range(4):
                tile_unit(u_in(2) + j, Z_Q + j // 2, j % 2)
                if j == 1:
                    dve.wait_ge(soft_ready, 3)
                    V.scalar_tensor_tensor(out=soft[:], in0=pre[:], scalar=0.0, in1=soft[:], op0=ALU.min,
                                           op1=ALU.subtract).then_inc(log_ready, 1)
            drains_after(2, 3)
            dve.wait_ge(aux.drained, FILL["dec", 3] + 1)
            dve.wait_ge(proj.drained, u_in(3))
            dve.wait_ge(x_lo_done, 16)
            level_diff(0)
            qk_product()
            for b in range(3, NB):
                for j in range(4):
                    lev = 2 * (b - 3) + j // 2
                    if j % 2 == 0 and b < 7 and lev:
                        level_diff(lev) if lev < len(LEVELS) else k_diff()
                    if b == 8 and j == 0:
                        dve.wait_ge(last_ready, 1)
                    if b in (5, 6):
                        v_unit(b, j)
                    else:
                        m, c = in_tile(b, j)
                        tile_unit(u_in(b) + j, Z_OF[b] + m, c)
                    if b == 8 and j in (1, 2):
                        o_var_of(j - 1)
                    if (b, j) == (8, 2):
                        dve.wait_ge(silu_ready, 6)
                    drains_after(b, j)
                    if (b, j) == (8, 1):
                        o_scale(0)
                    if (b, j) == (8, 2):
                        for n in range(4):
                            o_low(n)
                        o_scale(1)
                    if j % 2 == 0 and b < 7:
                        level_scale(lev) if lev < len(LEVELS) else k_scale()
                        if lev == NEAR:
                            near_product()
                    if (b, j) in ((5, 1), (5, 3), (6, 1), (6, 3)):
                        pooled(((5, 1), (5, 3), (6, 1), (6, 3)).index((b, j)))
                    if (b, j) == (7, 0):
                        dve.wait_ge(exp_b_ready, 1)
                        V.scalar_tensor_tensor(out=flat_q, in0=flat_q, scalar=DK ** -0.5, in1=scaled[:, 0, :],
                                               op0=ALU.mult, op1=ALU.mult).then_inc(q_ready, 1)
                        dve.wait_ge(q_ready, 1)

            dve.wait_ge(silu_ready, 8)
            drains_after(NB, 0)
            for n in range(4, 8):
                o_low(n)

            def f_feed(n):
                lo_tile(n, *out_tile(n), 1, f_hi, f_lo, f_hi_done, f_lo_done)
                add_squares(n, *out_tile(n), f_sq, f_sum)

            for n in range(16):
                m, c = out_tile(n)
                dve.wait_ge(x_back[m], 16)
                dve.wait_ge(proj.filled, U_OUT + n + 1)
                V.tensor_tensor(h[:, m, both(c)], h[:, m, both(c)], proj.bank(U_OUT + n)[:], ALU.add
                                ).then_inc(proj.drained, 1)
                if n:
                    f_feed(n - 1)
            f_feed(15)
            norm_stats(F_NORM2, 1)

            def ffn_pair(i, pair):
                ns = (2 * pair, 2 * pair + 1)
                for half, dst in enumerate((gate_t, up_t)):
                    for n in ns:
                        u = U_FFN + pair_order(n, half)
                        dve.wait_ge(proj.filled, i * 8 + (u + 1))
                        V.tensor_tensor(dst[:, n % 2, :], proj.bank(u)[:], rms_all[:, both(n % 2)], ALU.mult
                                        ).then_inc(proj.drained, 1)
                        if half == 0:
                            continue
                        dve.wait_ge(gate_silu, i * 4 + (n + 1))
                        dve.wait_ge(proj.drained, i * 8 + (u + 1))
                        V.tensor_tensor(up_t[:, n % 2, :], gate_t[:, n % 2, :], up_t[:, n % 2, :], ALU.mult
                                        ).then_inc(gu_ready, 1)
                        dve.wait_ge(gu_hi_ready, i * 4 + (n + 1))
                        V.tensor_tensor(gu_lo[:, pair, both(n % 2)], up_t[:, n % 2, :],
                                        gu_hi[:, pair, both(n % 2)].bitcast(F32), ALU.subtract).then_inc(gu_lo_ready, 1)

            def ffn_add(i, n):
                m, c = n % KT, n // KT
                dve.wait_ge(aux.filled, i * 16 + (F_DOWN + n + 1))
                V.tensor_tensor(h[:, m, both(c)], h[:, m, both(c)], aux.bank(F_DOWN + n)[:], ALU.add
                                ).then_inc(aux.drained, 1)

            with dve.Fori(0, GROUPS - 1) as i:
                for pair in range(2):
                    ffn_pair(i, pair)
                for n in range(16):
                    ffn_add(i, n)

            def e_low(n):
                lo_tile(n, n % KT, n // KT, 2, e_hi, e_lo, e_hi_done, e_lo_done)

            for pair in range(2):
                ffn_pair(GROUPS - 1, pair)
            for n in range(16):
                ffn_add(GROUPS - 1, n)
                if n:
                    e_low(n - 1)
            e_low(15)
            for k in range(PLE // P):
                dve.wait_ge(p_hi_done, k + 1)
                V.tensor_tensor(p_lo[:, k, :], p_raw[:, k, :], p_hi[:, k, :].bitcast(F32), ALU.subtract
                                ).then_inc(p_lo_done, 1)
            norm_var(F_NORM3, 0)
            norm_diag(2, 0)
            norm_take(F_NORM3, 0)
            norm_var(F_NORM3, 1)
            dve.wait_ge(aux.drained, F_NORM3 + 3)

            for pair in range(8):
                ns = (2 * pair, 2 * pair + 1)
                for n in ns:
                    if n == 1:
                        norm_diag(2, 1)
                        norm_take(F_NORM3, 1)
                        dve.wait_ge(aux.drained, F_NORM3 + 4)
                    u = U_PLE + pair_order(n, 0)
                    dve.wait_ge(proj.filled, u + 1)
                    V.tensor_tensor(ple_t[:, n % 2, :], proj.bank(u)[:], rms_all[:, both(ple_tile(n)[1])], ALU.mult
                                    ).then_inc(proj.drained, 1)
                    if n == 14:
                        norm_var(F_NORM4, 0)
                        norm_diag(3, 0)
                if pair == 7:
                    norm_take(F_NORM4, 0)
                for n in ns:
                    m, c = ple_tile(n)
                    u = U_PLE + pair_order(n, 1)
                    dve.wait_ge(proj.filled, u + 1)
                    dve.wait_ge(ple_sig, n + 1)
                    V.tensor_tensor(ple_t[:, n % 2, :], ple_t[:, n % 2, :], proj.bank(u)[:], ALU.mult
                                    ).then_inc(proj.drained, 1)
                    dve.wait_ge(proj.drained, u + 1)
                    V.tensor_tensor(h[:, m, both(c)], h[:, m, both(c)], ple_t[:, n % 2, :], ALU.add).then_inc(h_final, 1)
                for n in ns:
                    add_squares(n, *ple_tile(n), y_sq, y_sum)
            norm_var(F_NORM4, 1)
            norm_diag(3, 1)
            dve.wait_ge(aux.filled, F_NORM4 + NORM_FILLS)
            dve.wait_ge(h_gained, 16)
            for m in range(KT):
                V.tensor_tensor(h[:, m, both(1)], h[:, m, both(1)], aux.bank(F_NORM4 + 3)[:], ALU.mult).then_inc(y_second, 1)

        @block.tensor
        def _(pe):
            M = nc.tensor.matmul

            def split3(bank, w_h, w_l, x_h, x_l, start, stop):
                M(bank, w_h, x_h, start=start, stop=False)
                M(bank, w_h, x_l, start=False, stop=False)
                return M(bank, w_l, x_h, start=False, stop=stop)

            def unit(n, s, tiles, m, x_h, x_l, c, kts=KT, ready=None):
                wh = w_hi[s][:, 0:kts * tiles * P].rearrange("p (k n) -> p k n", k=kts)
                wl = w_lo[s][:, 0:kts * tiles * P].rearrange("p (k n) -> p k n", k=kts)
                cols = slice(m * P, (m + 1) * P)
                for k in range(kts):
                    if ready is not None:
                        ready(k)
                    i = split3(proj.bank(n)[:], wh[:, k, cols], wl[:, k, cols], x_h[:, k, both(c)], x_l[:, k, both(c)],
                               k == 0, k == kts - 1)
                i.then_inc(proj.filled, 1)

            def v_unit(n, s, j):
                wh, wl = (w[s][:].rearrange("p (k n) -> p k n", k=KT) for w in (w_hi, w_lo))
                for t in (2 * j, 2 * j + 1):
                    bank, rows = proj.bank(n)[:, (t % 2) * BW:(t % 2 + 1) * BW], slice(t * C, (t + 1) * C)
                    for k in range(KT):
                        i = split3(bank, a_hi[:, k, rows], a_lo[:, k, rows], wh[:, k, :], wl[:, k, :], k == 0, k == KT - 1)
                i.then_inc(proj.filled, 1)

            def token_sums(f0, c, ready):
                pe.wait_ge(*ready)
                aux.claim(f0 + 2 * c)
                for t in range(4):
                    i = M(aux.bank(f0 + 2 * c)[:, t:t + 1], sums[:, (4 * c + t) * P:(4 * c + t + 1) * P], ones[:, 0:1],
                          start=True, stop=True)
                i.then_inc(aux.filled, 1)

            def spread_rms(f0, norm, c):
                pe.wait_ge(diag_ready, 2 * norm + c + 1)
                aux.claim(f0 + 2 * c + 1)
                M(aux.bank(f0 + 2 * c + 1)[:], ones[:], sums[:, both(c)], start=True, stop=True).then_inc(aux.filled, 1)

            def fill(kind, n):
                f = FILL[kind, n]
                r, c = n % 2, n // 2
                rows = slice(r * DK, (r + 1) * DK)
                if kind == "o" and n == 0:
                    pe.wait_ge(kv_step, 9)
                    pe.wait_ge(aux.drained, f)
                elif kind == "o" or kind in range(NEAR) and n:
                    pass
                elif kind == "gate" and n == 0:
                    pe.wait_ge(proj.drained, 4)
                    pe.wait_ge(gate_w_landed, 16 * 3)
                elif kind == "dec" and n == 0:
                    pe.wait_ge(log_ready, 1)
                elif kind == "diag":
                    pe.wait_ge(qk_ready, 1)
                elif kind == "near":
                    pe.wait_ge(near_ready, 1)
                elif kind == "kt" and n == 0:
                    pe.wait_ge(scaled_ready, 2 * len(LEVELS) + 1)
                elif kind == "kv" and n == 0:
                    pe.wait_ge(aux.drained, FILL["kt", 3] + 1)
                elif kind == "y":
                    pe.wait_ge(pooled_ready, 2 * (n // NC) + 2)
                    pe.wait_ge(mixer_landed, 16 * 3)
                elif kind == "ot":
                    pe.wait_ge(o_scaled, 4 if n < 4 else 8)
                elif n == 0:
                    pe.wait_ge(scaled_ready, 2 * (kind + 1))
                aux.claim(f)
                bank = aux.bank(f)
                if kind == "gate":
                    for j in range(2):
                        t = 2 * n + j
                        i = M(bank[:, j * KEY:(j + 1) * KEY], lr[:, t * C:(t + 1) * C], w_gl[:], start=True, stop=True)
                elif kind == "dec":
                    for j in range(4):
                        i = M(bank[:, j * C:(j + 1) * C], soft[:, 4 * (n % 2) + j, (n // 2) * P:(n // 2 + 1) * P], tri[:],
                              start=True, stop=True)
                elif kind in ("diag", "near"):
                    sc = scaled[:, 1 if kind == "diag" else NEAR % 2, :].rearrange("p (a t c) -> p t a c", a=KP, c=C)
                    for j in range(NCH * KP):
                        i = M(bank[:, 2 * j:2 * j + 2], sc[:, j // KP, j % KP, :], head_ones[:], start=True, stop=True)
                elif kind == "kt":
                    for j in range(4):
                        t, a = 2 * n + j // 2, j % 2
                        i = nc.tensor.transpose(bank[:, j * P:(j + 1) * P], z[:, Z_K + a, t * C:(t + 1) * C], ident[:])
                elif kind == "kv":
                    for t in range(2 * n, min(2 * n + 2, NCH - 1)):
                        for a in range(KP):
                            for half in range(2):
                                col = ((t % 2) * KP + a) * DV
                                i = M(bank[half * DK:(half + 1) * DK, col:col + DV],
                                      k_tok[:, t, a * P + half * DK:a * P + (half + 1) * DK],
                                      v_tok[:, t, (2 * a + half) * DV:(2 * a + half + 1) * DV], start=True, stop=True)
                elif kind == "y":
                    g, c = n // NC, n % NC
                    i = M(bank[:], w_pl[:, g, :], z[:, Z_U + g, both(c)], start=True, stop=True)
                elif kind == "o":
                    for q in range(4):
                        t, a = 2 * c + q // 2, q % 2
                        o = bank[:, q * DV:(q + 1) * DV]
                        if t:
                            M(o, z[rows, Z_Q + a, t * C:(t + 1) * C], state[rows, t, a, :], start=True, stop=False)
                        i = M(o, attn[:, r, t, a, :], v_tok[:, t, (2 * a + r) * DV:(2 * a + r + 1) * DV],
                              start=t == 0, stop=True)
                elif kind == "ot":
                    c, hd = n // HEADS, n % HEADS
                    for j in range(4):
                        i = nc.tensor.transpose(bank[:, j * P:(j + 1) * P], o_tok[:, hd % 2, 4 * c + j, hd // 2, :], ident[:])
                else:
                    s = LEVELS[kind]
                    sc = scaled[:, kind % 2, :].rearrange("p (a t c) -> p a t c", a=KP, c=C)
                    for j in range(4 * KP):
                        t, a = 4 * c + j // KP, j % KP
                        right = sc[rows, a, t, :].rearrange("p (n s) -> p n s", s=2 * s)[:, :, s:2 * s]
                        i = M(bank[:, j * C // 2:(j + 1) * C // 2], sc[rows, a, t, :], right, start=True, stop=True)
                i.then_inc(aux.filled, 1)

            def fills_after(b, j):
                for kind, n in FILLS_AFTER.get((b, j), []):
                    fill(kind, n)

            pe.wait_ge(w_lo_ready[0], 1)
            pe.wait_ge(ones_ready, 5)
            for c in range(NC):
                proj.claim(3 * c)
                unit(3 * c, 0, 1, 0, a_hi, a_lo, c, ready=lambda k: pe.wait_ge(x_lo_done, KT * c + k + 1))
                if c == 0:
                    pe.wait_ge(first_lo, 1)
                    pe.wait_ge(w_lo_ready[1], 1)
                else:
                    token_sums(F_NORM1, c, (x_sum, 16))
                for m in range(2):
                    proj.claim(3 * c + 1 + m)
                    unit(3 * c + 1 + m, 1, 2, m, a_hi, a_lo, c)
                    if c == m == 0:
                        token_sums(F_NORM1, 0, (x_sum, 8))
                    if c != m:
                        spread_rms(F_NORM1, 0, c)
            fills_after(1, 3)
            for b in range(2, NB):
                s, n = slot_of(b)
                pe.wait_ge(w_lo_ready[s], n + 1)
                for j in range(4):
                    u = u_in(b) + j
                    proj.claim(u)
                    if b in (5, 6):
                        v_unit(u, s, j)
                    else:
                        m, c = in_tile(b, j)
                        unit(u, s, 2, m, a_hi, a_lo, c)
                    fills_after(b, j)

            def mix_ready(c):
                return lambda k: pe.wait_ge(o_lo, HEADS * c + k + 1) if k < HEADS else pe.wait_ge(y_lo, c + 1)

            for b in range(4):
                s, n = slot_of(NB + b)
                pe.wait_ge(w_lo_ready[s], n + 1)
                for j in range(4):
                    u = U_OUT + 4 * b + j
                    proj.claim(u)
                    m, c = out_tile(4 * b + j)
                    unit(u, s, BT, m % 2, mix_hi, mix_lo, c, ready=mix_ready(c) if b == 0 and m == 0 else None)
                    if b == 0:
                        fills_after(NB, j)

            wd_h = w_hi[S_DOWN][:].rearrange("p (k n) -> p k n", n=D)
            wd_l = w_lo[S_DOWN][:].rearrange("p (k n) -> p k n", n=D)

            def ffn_group(i, first=False):
                for pair in range(2):
                    for half, s in enumerate((S_GATE, S_UP)):
                        if pair == 0:
                            pe.wait_ge(w_lo_ready[s], i + (FFN_USE[s] + 1))
                        for c in range(NC):
                            u = U_FFN + pair_order(2 * pair + c, half)
                            opening = first and (pair, half) == (0, 0)
                            pe.wait_ge(proj.drained, i * 8 + (u - 3))
                            unit(u, s, BT, pair, f_hi, f_lo, c,
                                 ready=(lambda k: pe.wait_ge(f_lo_done, OUT_AT[k, c] + 1)) if opening else None)
                            if opening and c == 0:
                                token_sums(F_NORM2, 0, (f_sum, 15))
                            if opening and c == 1:
                                spread_rms(F_NORM2, 1, 0)
                                token_sums(F_NORM2, 1, (f_sum, 16))
                            if first and (pair, half, c) == (0, 1, 0):
                                spread_rms(F_NORM2, 1, 1)
                pe.wait_ge(w_lo_ready[S_DOWN], i + 1)
                for n in range(16):
                    m, c = n % KT, n // KT
                    if m == 0:
                        pe.wait_ge(gu_lo_ready, i * 4 + (3 + c))
                    pe.wait_ge(aux.drained, i * 16 + (F_DOWN + n - 3))
                    bank, cols = aux.bank(F_DOWN + n)[:], slice(m * P, (m + 1) * P)
                    for k in range(BT):
                        last_mm = split3(bank, wd_h[:, k, cols], wd_l[:, k, cols], gu_hi[:, k, both(c)],
                                         gu_lo[:, k, both(c)], k == 0, k == BT - 1)
                    last_mm.then_inc(aux.filled, 1)

            ffn_group(0, first=True)
            with pe.Fori(1, GROUPS) as i:
                ffn_group(i)

            for pair in range(8):
                b, ns = pair // 2, (2 * pair, 2 * pair + 1)
                s, use = ple_slot(b)
                pe.wait_ge(w_lo_ready[s], use + 1)
                for n in ns:
                    m, c = ple_tile(n)
                    u = U_PLE + pair_order(n, 0)
                    proj.claim(u)
                    unit(u, s, BT, m % 2, e_hi, e_lo, c,
                         ready=(lambda k: pe.wait_ge(e_lo_done, KT * n + k + 1)) if n < 2 else None)
                    if n == 0:
                        token_sums(F_NORM3, 0, (e_sum, 8))
                    if n == 1:
                        spread_rms(F_NORM3, 2, 0)
                        token_sums(F_NORM3, 1, (e_sum, 16))
                    if n == 14:
                        token_sums(F_NORM4, 0, (y_sum, 14))
                    if n == 15:
                        spread_rms(F_NORM4, 3, 0)
                pe.wait_ge(w_lo_ready[2], GROUPS + b + 1)
                if pair == 0:
                    pe.wait_ge(p_lo_done, PLE // P)
                for n in ns:
                    m, c = ple_tile(n)
                    u = U_PLE + pair_order(n, 1)
                    proj.claim(u)
                    unit(u, 2, BT, m % 2, p_hi, p_lo, c, kts=PLE // P)
                if pair == 0:
                    spread_rms(F_NORM3, 2, 1)
            token_sums(F_NORM4, 1, (y_sum, 16))
            spread_rms(F_NORM4, 3, 1)


_INS = ['x_t', 'p_t', 'gains_in', 'w_in', 'w_gate_lr', 'b_gate', 'w_pool', 'w_out', 'w_ffn_gate', 'w_ffn_up', 'w_ffn_down',
        'w_ple_gate', 'w_ple_proj', 'consts']
_OUTS = [((KT, P, T), 'float32')]


def laid_out(inputs):
    import numpy as np

    a = {n: np.asarray(v) for n, v in inputs.items()}

    def block(w, c0, n):
        return w[:, c0:c0 + n].reshape(-1, P, n).transpose(1, 0, 2).reshape(P, -1)

    def column_blocks(w):
        return np.stack([block(w, c, BW) for c in range(0, w.shape[1], BW)])

    return {
        'x_t': np.ascontiguousarray(a['x'][0].T).reshape(KT, P, T),
        'p_t': np.ascontiguousarray(a['p'][0, 0].T).reshape(PLE // P, P, T),
        'gains_in': np.concatenate([a[n].reshape(-1, P).T for n in
                                    ('ln_mix', 'ln_ffn', 'ln_ple', 'ln_final', 'pool_scale', 'gla_norm')], axis=1),
        'w_in': np.concatenate([block(a['w_in'][0], c0, tiles * P) for c0, tiles in BLOCKS_IN], axis=1),
        'w_gate_lr': a['w_gate_lr'], 'b_gate': a['b_gate'], 'w_pool': a['w_pool'],
        'w_out': column_blocks(a['w_out'][0]),
        'w_ffn_gate': column_blocks(a['w_ffn_gate'][0]),
        'w_ffn_up': column_blocks(a['w_ffn_up'][0]),
        'w_ffn_down': a['w_ffn_down'][0].reshape(GROUPS, BT, P, D).transpose(0, 2, 1, 3).reshape(GROUPS, P, BT * D),
        'w_ple_gate': column_blocks(a['w_ple_gate'][0]),
        'w_ple_proj': column_blocks(a['w_ple_proj'][0]),
        'consts': const_rows(),
    }


def kernel(**inputs):
    import numpy as _np
    import concourse.bacc as _bacc
    from concourse import mybir as _mybir
    from concourse.bass_utils import run_bass_kernel_spmd as _run

    nc = _bacc.Bacc("TRN2", target_bir_lowering=False, num_devices=1, dynamic_dma_scratch_size=1024)
    arrays, args = {}, []
    given = laid_out(inputs)
    for name in _INS:
        a = _np.ascontiguousarray(given[name])
        arrays[f"in_{name}_dram"] = a
        args.append(nc.dram_tensor(f"in_{name}_dram", a.shape, _mybir.dt.from_np(a.dtype), kind="ExternalInput").ap())
    for i, (shape, dtype) in enumerate(_OUTS):
        dt = _mybir.dt.from_np(_np.dtype(dtype))
        args.append(nc.dram_tensor(f"out_{i}_dram", shape, dt, kind="ExternalOutput").ap())
    hybrid_block(nc, *args)
    r = _run(nc, [arrays], core_ids=[0])
    got = tuple(r.results[0][f"out_{i}_dram"] for i in range(len(_OUTS)))
    return _np.ascontiguousarray(got[0].reshape(D, T).T).reshape(1, T, D)
```
